# Optimizing a Trainium2 kernel written in Bass

```python
import jax, jax.numpy as jnp
from jax import lax
import numpy as np

D_MODEL = 1024
BATCH = 1
SEQ = 1024
DEPTH = 1

CHUNK = 64
D_MIX = D_MODEL
ATT_HEADS = 8
ATT_KV_HEADS = 2
ATT_GROUP = ATT_HEADS // ATT_KV_HEADS
ATT_HEAD_DIM = 64
WINDOW = 128
WINDOW_CHUNKS = WINDOW // CHUNK
ML_HEADS = 4
ML_QK_DIM = 64
ML_V_DIM = 128
ML_CONV = 4
ML_F_BIAS_LO = 3.0
ML_F_BIAS_HI = 6.0
FFN_DIM = 2816
FFN_CONV = 3
EPS = 1e-6

ATT_Q_W = ATT_HEADS * ATT_HEAD_DIM
ATT_KV_W = ATT_KV_HEADS * ATT_HEAD_DIM
ML_QK_W = ML_HEADS * ML_QK_DIM
ML_V_W = ML_HEADS * ML_V_DIM
SPLIT_WIDTHS = (ATT_Q_W, ATT_KV_W, ATT_KV_W, ML_QK_W, ML_QK_W, ML_V_W, ML_V_W, ML_HEADS, ML_HEADS)
IN_W = ATT_Q_W + 2 * ATT_KV_W + 2 * ML_QK_W + 2 * ML_V_W + 2 * ML_HEADS
F_GATE_OFF = IN_W - ML_HEADS

kernel_name = 'hymba_swa_sink_mlstm_convffn'

def rmsnorm(x, g):
    x32 = x.astype(jnp.float32)
    y = x32 * lax.rsqrt(jnp.mean(x32 * x32, axis=-1, keepdims=True) + EPS)
    return (y * g.astype(jnp.float32)).astype(x.dtype)

def causal_dwconv(x, w, b):
    k = w.shape[0]
    s = x.shape[1]
    xp = jnp.pad(x, ((0, 0), (k - 1, 0), (0, 0)))
    out = b
    for j in range(k):
        out = out + xp[:, j:j + s, :] * w[j]
    return out

def shift_chunks(t, j):
    if j == 0:
        return t
    pad = [(0, 0), (j, 0)] + [(0, 0)] * (t.ndim - 2)
    return jnp.pad(t, pad)[:, :t.shape[1]]

def window_sink_attention(q, k, v, sinks):
    b, s, _ = q.shape
    nc = s // CHUNK
    q = q.reshape(b, nc, CHUNK, ATT_KV_HEADS, ATT_GROUP, ATT_HEAD_DIM)
    k = k.reshape(b, nc, CHUNK, ATT_KV_HEADS, ATT_HEAD_DIM)
    v = v.reshape(b, nc, CHUNK, ATT_KV_HEADS, ATT_HEAD_DIM)
    shifts = range(WINDOW_CHUNKS - 1, -1, -1)
    k_band = jnp.concatenate([shift_chunks(k, j) for j in shifts], axis=2)
    v_band = jnp.concatenate([shift_chunks(v, j) for j in shifts], axis=2)
    key_shift = np.repeat(np.arange(WINDOW_CHUNKS - 1, -1, -1), CHUNK)
    valid = jnp.arange(nc)[:, None] >= key_shift[None, :]
    scores = jnp.einsum('bnqkgd,bnskd->bnkgqs', q, k_band).astype(jnp.float32) * (ATT_HEAD_DIM ** -0.5)
    scores = jnp.where(valid[None, :, None, None, None, :], scores, -jnp.inf)
    sink = sinks.astype(jnp.float32).reshape(1, 1, ATT_KV_HEADS, ATT_GROUP, 1)
    lse = jnp.logaddexp(jax.nn.logsumexp(scores, axis=-1), sink)
    probs = jnp.exp(scores - lse[..., None]).astype(v.dtype)
    out = jnp.einsum('bnkgqs,bnskd->bnqkgd', probs, v_band)
    return out.reshape(b, s, ATT_Q_W)

def mlstm_chunkwise(q, k, v, i_pre, f_pre):
    b, s, _ = q.shape
    nc = s // CHUNK

    def heads(t, d):
        return t.astype(jnp.float32).reshape(b, nc, CHUNK, ML_HEADS, d).transpose(0, 3, 1, 2, 4)

    def gate(t):
        return t.astype(jnp.float32).reshape(b, nc, CHUNK, ML_HEADS).transpose(0, 3, 1, 2)

    q = heads(q, ML_QK_DIM)
    k = heads(k, ML_QK_DIM) * (ML_QK_DIM ** -0.5)
    v = heads(v, ML_V_DIM)
    log_i = gate(i_pre)
    log_f = jax.nn.log_sigmoid(gate(f_pre))
    cum_f = jnp.cumsum(log_f, axis=-1)
    tot_f = cum_f[..., -1]

    g = tot_f[..., None] - cum_f + log_i
    m_loc = jnp.max(g, axis=-1)
    w = jnp.exp(g - m_loc[..., None])
    c_loc = jnp.einsum('bhnl,bhnlk,bhnlv->bhnkv', w, k, v)
    n_loc = jnp.einsum('bhnl,bhnlk->bhnk', w, k)

    def step(carry, xs):
        c_st, n_st, m_st = carry
        c_l, n_l, m_l, f_l = xs
        m_new = jnp.maximum(f_l + m_st, m_l)
        a = jnp.exp(f_l + m_st - m_new)
        e = jnp.exp(m_l - m_new)
        c_new = a[..., None, None] * c_st + e[..., None, None] * c_l
        n_new = a[..., None] * n_st + e[..., None] * n_l
        return (c_new, n_new, m_new), (c_st, n_st, m_st)

    init = (jnp.zeros((b, ML_HEADS, ML_QK_DIM, ML_V_DIM), jnp.float32),
            jnp.zeros((b, ML_HEADS, ML_QK_DIM), jnp.float32),
            jnp.zeros((b, ML_HEADS), jnp.float32))
    xs = tuple(jnp.moveaxis(t, 2, 0) for t in (c_loc, n_loc, m_loc, tot_f))
    _, (c_prev, n_prev, m_prev) = lax.scan(step, init, xs)
    c_prev = jnp.moveaxis(c_prev, 0, 2)
    n_prev = jnp.moveaxis(n_prev, 0, 2)
    m_prev = jnp.moveaxis(m_prev, 0, 2)

    tri = jnp.tril(jnp.ones((CHUNK, CHUNK), dtype=bool))
    d = cum_f[..., :, None] - cum_f[..., None, :] + log_i[..., None, :]
    d = jnp.where(tri, d, -jnp.inf)
    m_t = jnp.maximum(cum_f + m_prev[..., None], jnp.max(d, axis=-1))
    s_qk = jnp.einsum('bhntk,bhnsk->bhnts', q, k) * jnp.exp(d - m_t[..., None])
    w_inter = jnp.exp(cum_f + m_prev[..., None] - m_t)
    num = (jnp.einsum('bhnts,bhnsv->bhntv', s_qk, v)
           + w_inter[..., None] * jnp.einsum('bhntk,bhnkv->bhntv', q, c_prev))
    den = jnp.sum(s_qk, axis=-1) + w_inter * jnp.einsum('bhntk,bhnk->bhnt', q, n_prev)
    h = num / jnp.maximum(jnp.abs(den), jnp.exp(-m_t))[..., None]
    return h.transpose(0, 2, 3, 1, 4).reshape(b, s, ML_V_W)

def hybrid_mixer(h, w_in, b_in, w_qk_conv, b_qk_conv, sinks, g_att, g_ml, w_out):
    z = h @ w_in + b_in
    idx = [int(i) for i in np.cumsum(SPLIT_WIDTHS)[:-1]]
    aq, ak, av, mq, mk, mv, mo, mi, mf = jnp.split(z, idx, axis=-1)
    mqk = jax.nn.silu(causal_dwconv(jnp.concatenate([mq, mk], axis=-1), w_qk_conv, b_qk_conv))
    mq, mk = jnp.split(mqk, 2, axis=-1)
    att = window_sink_attention(aq, ak, av, sinks)
    ml = mlstm_chunkwise(mq, mk, mv, mi, mf)
    ml = (jax.nn.sigmoid(mo.astype(jnp.float32)) * ml).astype(h.dtype)
    b, s, _ = h.shape
    att = rmsnorm(att, g_att)
    ml = rmsnorm(ml.reshape(b, s, ML_HEADS, ML_V_DIM), g_ml.reshape(ML_HEADS, ML_V_DIM)).reshape(b, s, ML_V_W)
    return jnp.concatenate([att, ml], axis=-1) @ w_out

def conv_ffn(h, w_up, w_conv, b_conv, w_down):
    u = causal_dwconv(h @ w_up, w_conv, b_conv)
    gate, up = jnp.split(u, 2, axis=-1)
    return (jax.nn.silu(gate) * up) @ w_down

def setup_inputs(seed: int = 0) -> dict:
    key = jax.random.key(seed)
    ks = jax.random.split(key, 16)
    f32 = jnp.float32

    def nrm(k, shape, scale):
        return jax.random.normal(k, shape, f32) * scale

    b_in = nrm(ks[3], (DEPTH, IN_W), 0.02)
    b_in = b_in.at[:, F_GATE_OFF:].add(jnp.linspace(ML_F_BIAS_LO, ML_F_BIAS_HI, ML_HEADS, dtype=f32))
    return {
        'x': nrm(ks[0], (BATCH, SEQ, D_MODEL), 1.0),
        'norm1_g': 1.0 + nrm(ks[1], (DEPTH, D_MODEL), 0.02),
        'w_in': nrm(ks[2], (DEPTH, D_MODEL, IN_W), D_MODEL ** -0.5),
        'b_in': b_in,
        'w_qk_conv': nrm(ks[4], (DEPTH, ML_CONV, 2 * ML_QK_W), ML_CONV ** -0.5),
        'b_qk_conv': nrm(ks[5], (DEPTH, 2 * ML_QK_W), 0.02),
        'attn_sinks': nrm(ks[6], (DEPTH, ATT_HEADS), 0.5),
        'g_att_out': 1.0 + nrm(ks[7], (DEPTH, ATT_Q_W), 0.02),
        'g_ml_out': 1.0 + nrm(ks[8], (DEPTH, ML_V_W), 0.02),
        'w_out': nrm(ks[9], (DEPTH, D_MIX, D_MODEL), D_MIX ** -0.5),
        'norm2_g': 1.0 + nrm(ks[10], (DEPTH, D_MODEL), 0.02),
        'w_up': nrm(ks[11], (DEPTH, D_MODEL, 2 * FFN_DIM), D_MODEL ** -0.5),
        'w_ffn_conv': nrm(ks[12], (DEPTH, FFN_CONV, 2 * FFN_DIM), FFN_CONV ** -0.5),
        'b_ffn_conv': nrm(ks[13], (DEPTH, 2 * FFN_DIM), 0.02),
        'w_down': nrm(ks[14], (DEPTH, FFN_DIM, D_MODEL), FFN_DIM ** -0.5),
        'final_g': 1.0 + nrm(ks[15], (D_MODEL,), 0.02),
    }

def reference(x, norm1_g, w_in, b_in, w_qk_conv, b_qk_conv, attn_sinks, g_att_out, g_ml_out,
              w_out, norm2_g, w_up, w_ffn_conv, b_ffn_conv, w_down, final_g):
    for l in range(DEPTH):
        h = rmsnorm(x, norm1_g[l])
        x = x + hybrid_mixer(h, w_in[l], b_in[l], w_qk_conv[l], b_qk_conv[l], attn_sinks[l],
                             g_att_out[l], g_ml_out[l], w_out[l])
        h = rmsnorm(x, norm2_g[l])
        x = x + conv_ffn(h, w_up[l], w_ffn_conv[l], b_ffn_conv[l], w_down[l])
    return rmsnorm(x, final_g)


_drawn_inputs = setup_inputs


def setup_inputs(seed=0):
    import zlib

    import numpy as np

    out = dict(_drawn_inputs(seed))
    spreads = {}
    factors = {'b_qk_conv': 4.654,
     'attn_sinks': 8.0,
     'g_att_out': 5.317,
     'g_ml_out': 5.47,
     'norm2_g': 5.164,
     'b_ffn_conv': 5.125,
     'final_g': 2.866}
    for name, (base, spread) in spreads.items():
        noise = np.random.default_rng([zlib.crc32(name.encode()), seed]).standard_normal(out[name].shape)
        drawn = base * np.exp(spread * noise) if base else spread * noise
        out[name] = __import__('jax').numpy.asarray(drawn.astype(out[name].dtype))
    for name, factor in factors.items():
        out[name] = (out[name] * factor).astype(out[name].dtype)
    return out
```

```python
from contextlib import ExitStack

import concourse.bass as bass
from concourse import mybir

ALU = mybir.AluOpType
ACT = mybir.ActivationFunctionType
AX_X = mybir.AxisListType.X
F32 = mybir.dt.float32
F32R = mybir.dt.float32r

P = 128
D = 1024
S = 1024
NK = D // P
NT = S // P
HALF = 512
CHUNK = 64
NC = S // CHUNK
EPS = 1e-6

ATT_HEADS = 8
KV_HEADS = 2
HD = 64
ML_HEADS = 4
ML_QK = 64
ML_V = 128
ATT_SCALE = HD ** -0.5
ML_SCALE = ML_QK ** -0.5
ML_TAPS = 4

F = 2816
FT = F // P
FFN_TAPS = 3
PAIRS = 2
GROUPS = FT // PAIRS

AQ, AK, AV, MQ, MK, MV, MO = 0, 4, 5, 6, 8, 10, 14
ZT = 18
GATES = ZT * P

VEC_ROWS = {}
_n = 0
for _name, _rows in (("b_in", ZT), ("g1", NK), ("g2", NK), ("g_att", 4), ("g_ml", ML_HEADS),
                     ("w_qk", 4 * ML_TAPS), ("b_qk", 4), ("b_ffn", 2 * FT)):
    VEC_ROWS[_name] = _n
    _n += _rows
VEC_A = _n
VEC_B = 2 * 2 * FT
VEC_C = 2 * FT
VECS = VEC_A + VEC_B + VEC_C

ROW_LOGF, ROW_CUM, ROW_CUM0, ROW_G, ROW_RESET, ROW_MAX, ROW_PREV, ROW_INTER, ROW_M, ROW_NEGMAX = range(1, 11)

SLOT = 4096
SLOTS = 51

RAW_COUNT = {}
_loads = [0, 0]
for _b in range(1, ZT + 1):
    _loads[_b % 2] += 32 if _b <= 4 else 16
    RAW_COUNT[_b] = _loads[_b % 2]
WO_COUNT = {}
_loads = [0, 0]
for _k in range(NK):
    _loads[(_k + 1) % 2] += 32 if _k < 4 else 16
    WO_COUNT[_k] = _loads[(_k + 1) % 2]


def hymba_kernel(nc, x, norm1_g, w_in, b_in, w_qk_conv, b_qk_conv, attn_sinks, g_att_out, g_ml_out,
                 w_out, norm2_g, w_up, w_ffn_conv, b_ffn_conv, w_down, final_g, out):
    x_d = x.rearrange("a s d -> (a s) d")
    out_d = out.rearrange("a s d -> (a s) d")
    w_in_d = w_in.rearrange("l (k p) n -> p (l k) n", p=P)
    w_out_d = w_out.rearrange("l k n -> (l k) n")
    w_up_d = w_up.rearrange("l (k p) n -> p (l k) n", p=P)
    w_down_d = w_down.rearrange("l (k p) n -> p (l k) n", p=P)

    negmax_d = nc.dram_tensor("negmax_rows", (ML_HEADS, S), F32, kind="Internal").ap()
    inter_d = nc.dram_tensor("inter_rows", (ML_HEADS, S), F32, kind="Internal").ap()

    with ExitStack() as ctx:
        def sb(name, shape, dt=F32):
            return ctx.enter_context(nc.sbuf_tensor(name, shape, dt))

        def sem(name):
            return ctx.enter_context(nc.semaphore(name))

        base = -(-nc.sbuf_base // 32) * 32
        sb("arena", [P, SLOTS * SLOT // 4])

        def at(slot, name, shape, dt=F32, extra=0):
            return nc.alloc_sbuf_tensor_at(name, [P, *shape], dt, offset=base + slot * SLOT + extra)

        h_hi = at(0, "h_hi", [NK, S], F32R)
        h_lo = at(8, "h_lo", [NK, S], F32R)
        wo_hi = at(0, "wo_hi", [NK, D], F32R)
        wo_lo = at(8, "wo_lo", [NK, D], F32R)
        act_hi = at(0, "act_hi", [PAIRS, S], F32R)
        act_lo = at(2, "act_lo", [PAIRS, S], F32R)
        conv_g = at(4, "conv_g", [PAIRS, S])
        conv_u = at(6, "conv_u", [PAIRS, S])
        wd_hi = at(8, "wd_hi", [PAIRS, D], F32R)
        wd_lo = at(10, "wd_lo", [PAIRS, D], F32R)

        z = at(16, "z", [ZT, S])
        zq = at(16, "zq", [NC, 4, CHUNK])
        x_in = at(16, "x_in", [NT, D])
        x_hat = at(24, "x_hat", [NT, D])
        junk0 = at(32, "junk0", [D])
        row_a = at(30, "row_a", [S])
        row_b = at(31, "row_b", [S])
        row_c = at(32, "row_c", [S])
        row_d = at(33, "row_d", [S])
        h2_hi_a = at(20, "h2_hi_a", [6, S], F32R)
        h2_b = at(30, "h2_b", [4, S], F32R)
        h2_lo_a = at(43, "h2_lo_a", [6, S], F32R)

        raw = at(34, "raw", [2, D])
        w_hi = [at(36 + 2 * s, f"w_hi{s}", [D], F32R) for s in range(2)]
        w_lo = [at(37 + 2 * s, f"w_lo{s}", [D], F32R) for s in range(2)]
        mix_hi = [at(36 + 2 * s, f"mix_hi{s}", [NK, P], F32R) for s in range(2)]
        mix_lo = [at(37 + 2 * s, f"mix_lo{s}", [NK, P], F32R) for s in range(2)]
        att_v = at(36, "att_v", [NC, P])
        ml_v = at(36, "ml_v", [2, ML_HEADS, ML_V + 1])
        ml_k = at(38, "ml_k", [2, ML_HEADS * ML_QK])
        ml_p = at(39, "ml_p", [2, 2, 2, P])

        probs = at(40, "probs", [2, 4, P])
        probs_t = at(41, "probs_t", [2, 4, P])
        junk2 = at(42, "junk2", [512], extra=2048)
        x_again = at(40, "x_again", [2, D])
        x_hat2 = at(42, "x_hat2", [D])

        decay = at(43, "decay", [ML_HEADS, S])
        qk_acc = at(47, "qk_acc", [S])
        reset = at(47, "reset", [S])
        qk_sig = at(48, "qk_sig", [S])
        ml_t = at(47, "ml_t", [2, ML_HEADS, P])
        gates_t = at(48, "gates_t", [NT, 36], extra=2080)
        gate_w = at(40, "gate_w", [NK, 2 * ML_HEADS])
        pair_rows = at(41, "pair_rows", [2, P])
        state = at(48, "state", [2, 2, ML_V + 1])
        q_inter = at(49, "q_inter", [2, S])
        h2_f = at(49, "h2_f", [NK, P])
        final_gb = at(50, "final_gb", [D])
        vec_rows = at(49, "vec_rows", [3, P])
        ysq = at(34, "ysq", [D])
        y = [at(s, f"y{n}", [D]) for n, s in enumerate([20, 21, 22, 23, 24, 25, 30, 31])]

        ident = sb("ident", [P, P])
        fold = sb("fold", [P, P])
        vec = sb("vec", [P, VECS])
        gate_b = sb("gate_b", [P, 1])
        eps = sb("eps", [P, 1])
        one = sb("one", [P, 1])
        ssq = sb("ssq", [P, NT])
        root = sb("root", [P, NT])
        rstd = sb("rstd", [P, NT])
        m_prev = sb("m_prev", [ML_HEADS, NT])
        carry = sb("carry", [P, 2, NT])
        sinks = sb("sinks", [P, ATT_HEADS])
        sink = sb("sink", [P, 4])
        neg_sink = sb("neg_sink", [P, 4])
        top = sb("top", [P, 2, 4])
        neg_top = sb("neg_top", [P, 2, 4])
        sink_arg = sb("sink_arg", [P, 2, 4])
        sink_e = sb("sink_e", [P, 2, 4])
        total = sb("total", [P, 2, 4])
        total1 = sb("total1", [P, 2, 4])
        inv = sb("inv", [P, 2, 4])
        den = sb("den", [P, 2, 4])
        inv_den = sb("inv_den", [P, 2, 4])
        sq_att = sb("sq_att", [P, NC])
        sq_ml = sb("sq_ml", [P, NT, ML_HEADS])
        r_att0 = sb("r_att0", [P, NC])
        r_ml0 = sb("r_ml0", [P, NT * ML_HEADS])
        r_att = sb("r_att", [P, NC])
        r_ml = sb("r_ml", [P, NT, ML_HEADS])
        ss2 = sb("ss2", [P, NT, 2])
        ms2 = sb("ms2", [P, NT])
        ss3 = sb("ss3", [P, NT, 2])
        ms3 = sb("ms3", [P, NT])

        def column(name, n, k=1):
            c = VEC_ROWS[name] + n
            return vec[:, c:c + k]

        pz = [ctx.enter_context(nc.psum_tensor(f"pz{s}", [P, 2 * HALF], F32)) for s in range(2)]
        pd = [ctx.enter_context(nc.psum_tensor(f"pd{s}", [P, HALF], F32)) for s in range(4)]
        bank = [pz[0][:, 0:HALF], pz[0][:, HALF:], pz[1][:, 0:HALF], pz[1][:, HALF:]] + [p[:, :] for p in pd]

        names = """vec_loaded small_loaded gate_w_loaded const_made mem_made vec_turned vec_ready
            x_squared x_mean x_rooted x_rstd x_scaled x_turned h_hi_made h_lo_made
            gate_w_cleared gate_w_spread z_hi_made z_split z_done z_evac
            gi_ready gf_ready f_abs f_exp f_ln row_step inter_made floor_made rows_stored rows_spread
            gates_turned gates_t_ready carry_ready decay_arg decay_exp decay_made
            qk_acc_made qk_tap qk_sig_made qk_made q_inter_made
            wo_hi_made wo_split
            att_scored att_topped att_exped att_summed att_scaled att_v_turned att_v_made
            att_p_turned att_p_made att_done att_kept att_squared dve_step
            ml_scored ml_k_turned ml_v_turned ml_o_turned ml_summed ml_stated
            ml_v_made ml_k_made ml_p_made ml_state_made ml_den ml_inv ml_divided ml_kept ml_squared ml_ones
            att_folded norm_rooted norm_made
            mix_scaled mix_turned mix_hi_made mix_lo_made out_done x1_added x1_squared x1_mean x1_rooted
            x1_rstd x1_scaled h2_turned h2_f_made h2_hi_made h2_lo_made
            ffn_hi_made ffn_split up_done conv_first conv_tap conv_made silu_made prod_made
            act_hi_made act_split down_done down_added final_g_loaded
            x2_squared x2_mean x2_rooted x2_rstd y_made y_stored""".split()
        s = {n: sem(n) for n in names}
        x_loaded = [sem(f"x_loaded{i}") for i in range(NT)]
        x_reloaded = [sem(f"x_reloaded{i}") for i in range(2)]
        raw_loaded = [sem(f"raw_loaded{i}") for i in range(2)]
        wo_loaded = [sem(f"wo_loaded{i}") for i in range(2)]
        ffn_loaded = [sem(f"ffn_loaded{i}") for i in range(2)]

        block = ctx.enter_context(nc.Block())

        def keys(n):
            return (0, CHUNK) if n == 0 else ((n - 1) * CHUNK, 2 * CHUNK)

        def x1(i, half):
            if half == 0:
                return zq[:, 2 * i:2 * i + 2, :, :].rearrange("p n j d -> p (n j d)").rearrange("p (c t) -> p c t", c=4)
            return z[:, MV:MV + 4, i * P:(i + 1) * P]

        def h2(part, k):
            if k < 6:
                return (h2_hi_a, h2_lo_a)[part][:, k, :]
            return h2_b[:, 2 * part + k - 6, :]

        @block.sync
        def _(sp):
            for i in range(NT):
                sp.dma_start(x_in[:, i, :], x_d[i * P:(i + 1) * P, :]).then_inc(x_loaded[i], 16)
            for b in range(1, ZT + 1):
                j = b - 1
                if b >= 2:
                    sp.wait_ge(s["z_split"], b - 1)
                dst = raw[:, b % 2, :].rearrange("p (k n) -> p k n", k=NK)
                if j < 4:
                    for kv in range(KV_HEADS):
                        c = (j + 4 * kv) * HD
                        sp.dma_start(dst[:, :, kv * HD:(kv + 1) * HD], w_in_d[:, :, c:c + HD])\
                          .then_inc(raw_loaded[b % 2], 16)
                else:
                    sp.dma_start(dst, w_in_d[:, :, j * P:(j + 1) * P]).then_inc(raw_loaded[b % 2], 16)
            for k in range(NK):
                if k < 2:
                    sp.wait_ge(s["z_split"], ZT + k)
                else:
                    sp.wait_ge(s["wo_split"], k - 1)
                if k < 4:
                    kv, a = k // 2, k % 2
                    for pp in range(2):
                        r = (kv * 4 + 2 * pp + a) * HD
                        sp.dma_start(raw[pp * HD:(pp + 1) * HD, (k + 1) % 2, :], w_out_d[r:r + HD, :])\
                          .then_inc(wo_loaded[(k + 1) % 2], 16)
                else:
                    r = 512 + (k - 4) * P
                    sp.dma_start(raw[:, (k + 1) % 2, :], w_out_d[r:r + P, :]).then_inc(wo_loaded[(k + 1) % 2], 16)
            for i in range(NT):
                if i < 2:
                    sp.wait_ge(s["norm_made"], 1)
                else:
                    sp.wait_ge(s["x1_added"], 2 * (i - 1))
                sp.dma_start(x_again[:, i % 2, :], x_d[i * P:(i + 1) * P, :]).then_inc(x_reloaded[i % 2], 16)

            def up_tile(c):
                return w_up_d[:, :, bass.ds(c * P, P)]

            def load_up(slot, c):
                sp.dma_start(raw[:, slot, :].rearrange("p (k n) -> p k n", k=NK), up_tile(c))\
                  .then_inc(ffn_loaded[slot], 16)

            def load_group(g, last):
                sp.wait_ge(s["ffn_split"], 6 * g + 1)
                load_up(0, 2 * g + 1)
                sp.wait_ge(s["ffn_split"], 6 * g + 2)
                load_up(1, FT + 2 * g + 1)
                for m in range(PAIRS):
                    sp.wait_ge(s["ffn_split"], 6 * g + 3 + m)
                    sp.dma_start(raw[:, m, :], w_down_d[:, bass.ds(2 * g + m, 1), :]).then_inc(ffn_loaded[m], 16)
                if not last:
                    sp.wait_ge(s["ffn_split"], 6 * g + 5)
                    load_up(0, 2 * g + 2)
                    sp.wait_ge(s["ffn_split"], 6 * g + 6)
                    load_up(1, FT + 2 * g + 2)

            sp.wait_ge(s["ml_summed"], NT)
            sp.dma_start(final_gb[:, :], final_g.partition_broadcast(P)).then_inc(s["final_g_loaded"], 16)
            sp.wait_ge(s["wo_split"], NK)
            load_up(0, 0)
            load_up(1, FT)
            with sp.Fori(0, GROUPS - 1) as g:
                load_group(g, False)
            load_group(GROUPS - 1, True)
            for i in range(NT):
                sp.wait_ge(s["y_made"], i + 1)
                sp.dma_start(out_d[i * P:(i + 1) * P, :], y[i][:, :]).then_inc(s["y_stored"], 16)
            sp.wait_ge(s["y_stored"], 16 * NT)

        @block.gpsimd
        def _(pool):
            nc.gpsimd.memset(ident[:, :], 0.0).then_inc(s["mem_made"], 1)
            nc.gpsimd.memset(fold[:, :], 0.0).then_inc(s["mem_made"], 1)
            nc.gpsimd.memset(pair_rows[0:ML_HEADS, :, :], 1.0).then_inc(s["mem_made"], 1)
            pool.wait_ge(s["mem_made"], 1)
            nc.gpsimd.affine_select(out=ident[:, :], in_=ident[:, :], compare_op=ALU.not_equal, fill=1.0,
                                    base=0, pattern=[[-1, P]], channel_multiplier=1).then_inc(s["const_made"], 1)
            for kv in range(KV_HEADS):
                pool.dma_start(vec_rows[0:4, 0, kv * HD:(kv + 1) * HD],
                               b_in[0, kv * 4 * HD:(kv + 1) * 4 * HD].rearrange("(c d) -> c d", d=HD))\
                    .then_inc(s["vec_loaded"], 16)
            pool.dma_start(vec_rows[4:ZT, 0, :], b_in[0, 4 * P:ZT * P].rearrange("(n p) -> n p", p=P))\
                .then_inc(s["vec_loaded"], 16)
            r = VEC_ROWS
            for name, src in (("g1", norm1_g), ("g2", norm2_g), ("g_ml", g_ml_out), ("b_qk", b_qk_conv),
                              ("b_ffn", b_ffn_conv)):
                rows = src.shape[1] // P
                pool.dma_start(vec_rows[r[name]:r[name] + rows, 0, :], src[0, :].rearrange("(n p) -> n p", p=P))\
                    .then_inc(s["vec_loaded"], 16)
            ga = g_att_out[0, :].rearrange("(v u a d) -> v a u d", v=2, u=2, a=2)
            for kv in range(2):
                pool.dma_start(vec_rows[r["g_att"] + 2 * kv:r["g_att"] + 2 * kv + 2, 0, :]
                               .rearrange("a (u d) -> a u d", u=2), ga[kv]).then_inc(s["vec_loaded"], 16)
            pool.dma_start(vec_rows[r["w_qk"]:r["w_qk"] + 4 * ML_TAPS, 0, :],
                           w_qk_conv[0].rearrange("t (n p) -> (t n) p", p=P)).then_inc(s["vec_loaded"], 16)
            for t in range(FFN_TAPS):
                row = t % 2 * 2 * FT
                pool.dma_start(vec_rows[row:row + 2 * FT, 1 + t // 2, :],
                               w_ffn_conv[0, t, :].rearrange("(n p) -> n p", p=P)).then_inc(s["vec_loaded"], 16)
            pool.dma_start(gate_w[:, :, :], w_in_d[:, :, GATES:GATES + 2 * ML_HEADS]).then_inc(s["gate_w_loaded"], 16)
            for a, col in ((0, 0), (32, ML_HEADS)):
                pool.dma_start(gate_b[a:a + ML_HEADS, :], b_in[0, GATES + col:GATES + col + ML_HEADS]
                               .rearrange("(n a) -> n a", a=1)).then_inc(s["small_loaded"], 16)
            pool.dma_start(sinks[:, :], attn_sinks[0, :].partition_broadcast(P)).then_inc(s["small_loaded"], 16)
            nc.gpsimd.memset(eps[:, :], EPS).then_inc(s["mem_made"], 1)
            nc.gpsimd.memset(one[:, :], 1.0).then_inc(s["mem_made"], 1)
            nc.gpsimd.memset(raw[:, 0, :], 0.0).then_inc(s["gate_w_cleared"], 1)
            nc.gpsimd.memset(reset[:, :], 1.0).then_inc(s["mem_made"], 1)
            nc.gpsimd.memset(m_prev[:, :], 0.0).then_inc(s["mem_made"], 1)
            pool.wait_ge(s["mem_made"], 7)
            nc.gpsimd.memset(reset[:, 0:S:P], 0.0).then_inc(s["const_made"], 1)
            for n, off in enumerate((0, 64, -64)):
                if n:
                    pool.wait_ge(s["const_made"], 2 + n)
                nc.gpsimd.affine_select(out=fold[:, :], in_=fold[:, :], compare_op=ALU.not_equal, fill=1.0,
                                        base=off, pattern=[[-1, P]], channel_multiplier=1)\
                    .then_inc(s["const_made"], 1)
            nc.gpsimd.affine_select(out=pair_rows[0:ML_HEADS, :, :].rearrange("h r (e d) -> h r e d", e=2),
                                    in_=pair_rows[0:ML_HEADS, :, :].rearrange("h r (e d) -> h r e d", e=2),
                                    compare_op=ALU.is_equal, fill=0.0, base=0,
                                    pattern=[[-2, 2], [-1, 2], [0, 64]], channel_multiplier=1)\
                .then_inc(s["const_made"], 1)
            pool.wait_ge(s["x_turned"], 16)
            nc.gpsimd.memset(row_a[0:36, :], 0.0).then_inc(s["const_made"], 1)
            nc.gpsimd.memset(row_c[0:ML_HEADS, :], 0.0).then_inc(s["const_made"], 1)
            pool.wait_ge(s["inter_made"], 1)
            pool.dma_start(inter_d, row_c[0:ML_HEADS, :]).then_inc(s["rows_stored"], 16)
            pool.wait_ge(s["row_step"], ROW_NEGMAX)
            pool.dma_start(negmax_d, row_d[0:ML_HEADS, :]).then_inc(s["rows_stored"], 16)
            pool.wait_ge(s["rows_stored"], 32)
            for h in range(ML_HEADS):
                pool.dma_start(decay[:, h, :], negmax_d[h, :].partition_broadcast(P))\
                  .then_inc(s["rows_spread"], 16)
                pool.dma_start(q_inter[(h % 2) * 64:(h % 2) * 64 + 64, h // 2, :],
                             inter_d[h, :].partition_broadcast(64)).then_inc(s["rows_spread"], 16)
            for i in range(NT):
                pool.wait_ge(s["decay_exp"], i + 1)
                d = decay[:, :, i * P:(i + 1) * P]
                nc.gpsimd.affine_select(out=d, in_=d, compare_op=ALU.is_ge, fill=0.0, base=0,
                                        pattern=[[0, ML_HEADS], [1, P]], channel_multiplier=-1)\
                    .then_inc(s["decay_made"], 1)
            for n in range(NC):
                _, kw = keys(n)
                pool.wait_ge(s["att_summed"], 3 * n + 3)
                p = probs[:, n % 2, :, 0:kw]
                nc.gpsimd.tensor_tensor(p, p, inv[:, n % 2, :].unsqueeze(2).to_broadcast([P, 4, kw]), ALU.mult)\
                    .then_inc(s["att_scaled"], 1)

        @block.scalar
        def _(act):
            act.wait_ge(s["mem_made"], 5)
            for i in range(NT):
                act.wait_ge(x_loaded[i], 16)
                nc.scalar.activation(junk0[:, :], x_in[:, i, :], ACT.Square, accum_out=ssq[:, i:i + 1])\
                    .then_inc(s["x_squared"], 1)
                act.wait_ge(s["x_squared"], i + 1)
                nc.scalar.activation(root[:, i:i + 1], ssq[:, i:i + 1], ACT.Sqrt, bias=eps[:, :], scale=1.0 / D)\
                    .then_inc(s["x_rooted"], 1)
            act.wait_ge(s["vec_ready"], 1)

            def h_high(n):
                half, k = n // NK, n % NK
                act.wait_ge(s["x_turned"], n + 1)
                nc.scalar.activation(h_hi[:, k, half * HALF:(half + 1) * HALF], bank[k], ACT.Copy,
                                     scale=column("g1", k)).then_inc(s["h_hi_made"], 1)

            for n in range(NK):
                h_high(n)

            def weight_high(b):
                if b == 0:
                    act.wait_ge(s["gate_w_spread"], 2)
                else:
                    act.wait_ge(raw_loaded[b % 2], RAW_COUNT[b])
                if b >= 2:
                    act.wait_ge(s["z_done"], b - 1)
                nc.scalar.activation(w_hi[b % 2][:, :], raw[:, b % 2, :], ACT.Copy).then_inc(s["z_hi_made"], 1)

            weight_high(0)
            weight_high(1)
            for n in range(NK, 2 * NK):
                h_high(n)

            for b in range(ZT + 1):
                if b + 2 <= ZT:
                    weight_high(b + 2)
                act.wait_ge(s["z_done"], b + 1)
                src = pz[b % 2]
                if b == 0:
                    act.wait_ge(s["const_made"], 8)
                    act.wait_ge(s["small_loaded"], 48)
                    nc.scalar.activation(row_a[0:ML_HEADS, :], src[0:ML_HEADS, :], ACT.Identity,
                                         bias=gate_b[0:ML_HEADS, :]).then_inc(s["gi_ready"], 1)
                    nc.scalar.activation(row_b[32:36, :], src[32:36, :], ACT.Identity,
                                         bias=gate_b[32:36, :]).then_inc(s["z_evac"], 1)
                    act.wait_ge(s["z_evac"], 1)
                    nc.scalar.activation(row_c[32:36, :], row_b[32:36, :], ACT.Abs).then_inc(s["f_abs"], 1)
                    act.wait_ge(s["f_abs"], 1)
                    nc.scalar.activation(row_c[32:36, :], row_c[32:36, :], ACT.Exp, scale=-1.0).then_inc(s["f_exp"], 1)
                    act.wait_ge(s["f_exp"], 1)
                    nc.scalar.activation(row_c[32:36, :], row_c[32:36, :], ACT.Ln, bias=one[32:36, :])\
                        .then_inc(s["f_ln"], 1)
                    continue
                j = b - 1
                if j == 1:
                    act.wait_ge(s["row_step"], ROW_INTER)
                    nc.scalar.activation(row_c[0:ML_HEADS, :], row_c[0:ML_HEADS, :], ACT.Exp)\
                        .then_inc(s["inter_made"], 1)
                    act.wait_ge(s["row_step"], ROW_M)
                    nc.scalar.activation(row_a[32:36, :], row_b[0:ML_HEADS, :], ACT.Exp, scale=-1.0)\
                        .then_inc(s["floor_made"], 1)
                if j >= MO:
                    if j == MO:
                        act.wait_ge(s["rows_stored"], 32)
                        act.wait_ge(s["gates_turned"], 2)
                        act.wait_ge(s["row_step"], ROW_NEGMAX)
                    nc.scalar.activation(z[:, j, :], src[:, :], ACT.Sigmoid, bias=column("b_in", j))\
                        .then_inc(s["z_evac"], 1)
                elif j < AK:
                    nc.scalar.activation(zq[:, :, j, :], src[:, :].rearrange("p (n t) -> p n t", t=CHUNK),
                                         ACT.Identity, bias=column("b_in", j)).then_inc(s["z_evac"], 1)
                else:
                    nc.scalar.activation(z[:, j, :], src[:, :], ACT.Identity, bias=column("b_in", j))\
                        .then_inc(s["z_evac"], 1)
                if MQ < j <= MV:
                    n = j - 1 - MQ
                    act.wait_ge(s["qk_tap"], ML_TAPS * (n + 1))
                    if n:
                        act.wait_ge(s["qk_made"], n)
                    nc.scalar.activation(qk_sig[:, :], qk_acc[:, :], ACT.Sigmoid).then_inc(s["qk_sig_made"], 1)
                if j == MV + 1:
                    for i in range(NT):
                        act.wait_ge(s["decay_arg"], ML_HEADS * (i + 1))
                        d = decay[:, :, i * P:(i + 1) * P]
                        nc.scalar.activation(d, d, ACT.Exp).then_inc(s["decay_exp"], 1)

            def att_exps(n):
                _, kw = keys(n)
                act.wait_ge(s["att_topped"], 3 * n + 3)
                if n >= 2:
                    act.wait_ge(s["att_p_turned"], n - 1)
                for j in range(4):
                    sc = pz[n % 2][:, (j // 2) * HALF + (j % 2) * P:(j // 2) * HALF + (j % 2) * P + kw]
                    nc.scalar.activation(probs[:, n % 2, j, 0:kw], sc, ACT.Exp,
                                         bias=neg_top[:, n % 2, j:j + 1], scale=ATT_SCALE,
                                         accum_out=total[:, n % 2, j:j + 1])
                nc.scalar.activation(sink_e[:, n % 2, :], sink_arg[:, n % 2, :], ACT.Exp).then_inc(s["att_exped"], 1)

            def att_v_keep(c):
                act.wait_ge(s["att_v_turned"], c + 1)
                nc.scalar.activation(att_v[:, 4 * c:4 * c + 4, :], bank[4 + c].rearrange("p (n d) -> p n d", n=4),
                                     ACT.Copy).then_inc(s["att_v_made"], 1)

            def att_square(n):
                act.wait_ge(s["att_kept"], n + 1)
                if n >= 2:
                    act.wait_ge(s["att_squared"], n - 1)
                nc.scalar.activation(junk2[:, n % 2 * 256:(n % 2 + 1) * 256].rearrange("p (j d) -> p j d", j=4), zq[:, n, :, :], ACT.Square,
                                     accum_out=sq_att[:, n:n + 1]).then_inc(s["att_squared"], 1)

            def wo_high(k):
                act.wait_ge(wo_loaded[(k + 1) % 2], WO_COUNT[k])
                gain = column("g_att", k) if k < 4 else column("g_ml", k - 4)
                nc.scalar.activation(wo_hi[:, k, :], raw[:, (k + 1) % 2, :], ACT.Copy, scale=gain)\
                    .then_inc(s["wo_hi_made"], 1)

            for c in range(4):
                att_v_keep(c)
            for n in range(NC + 3):
                if n < NC:
                    att_exps(n)
                if n % 2 == 1 and n // 2 < NK:
                    wo_high(n // 2)
                if n >= 3:
                    att_square(n - 3)

            def ml_v_keep(i):
                act.wait_ge(s["ml_v_turned"], i + 1)
                act.wait_ge(s["ml_ones"], 1)
                if i >= 2:
                    act.wait_ge(s["ml_stated"], i - 1)
                nc.scalar.activation(ml_v[:, i % 2, :, 0:ML_V], bank[5].rearrange("p (h d) -> p h d", h=ML_HEADS),
                                     ACT.Copy).then_inc(s["ml_v_made"], 1)

            def ml_square(i):
                act.wait_ge(s["ml_kept"], i + 1)
                if i:
                    act.wait_ge(s["ml_squared"], i)
                else:
                    act.wait_ge(s["att_squared"], NC)
                for h in range(ML_HEADS):
                    last = nc.scalar.activation(junk2[:, h * P:(h + 1) * P], z[:, MV + h, i * P:(i + 1) * P], ACT.Square,
                                                accum_out=sq_ml[:, i, h:h + 1])
                last.then_inc(s["ml_squared"], 1)

            for i in range(NT + 1):
                if i < NT:
                    ml_v_keep(i)
                if i >= 1:
                    ml_square(i - 1)

            act.wait_ge(s["ml_squared"], NT)
            nc.scalar.activation(r_ml0[:, :], sq_ml[:, :, :].rearrange("p i h -> p (i h)"), ACT.Sqrt,
                                 bias=eps[:, :], scale=1.0 / ML_V)
            act.wait_ge(s["att_folded"], 1)
            nc.scalar.activation(r_att0[:, :], bank[4][:, 0:NC], ACT.Sqrt, bias=eps[:, :],
                                 scale=1.0 / (ATT_HEADS * HD)).then_inc(s["norm_rooted"], 1)

            def mix_high(i):
                act.wait_ge(s["mix_turned"], i + 1)
                if i >= 2:
                    act.wait_ge(s["out_done"], 2 * (i - 1))
                nc.scalar.activation(mix_hi[i % 2][:, :, :].rearrange("p k t -> p (k t)"), pz[0][:, :], ACT.Copy)\
                    .then_inc(s["mix_hi_made"], 1)

            def h2_high(i):
                act.wait_ge(s["h2_f_made"], i + 1)
                t = slice(i * P, (i + 1) * P)
                nc.scalar.activation(h2_hi_a[:, :, t], h2_f[:, 0:6, :], ACT.Copy)
                nc.scalar.activation(h2_b[:, 0:2, t], h2_f[:, 6:8, :], ACT.Copy).then_inc(s["h2_hi_made"], 1)

            def x1_square(i):
                for half in range(2):
                    act.wait_ge(s["x1_added"], 2 * i + half + 1)
                    last = nc.scalar.activation(x_hat2[:, half * HALF:(half + 1) * HALF]
                                                .rearrange("p (c t) -> p c t", c=4), x1(i, half), ACT.Square,
                                                accum_out=ss2[:, i, half:half + 1])
                last.then_inc(s["x1_squared"], 1)
                act.wait_ge(s["x1_mean"], i + 1)
                nc.scalar.activation(root[:, i:i + 1], ms2[:, i:i + 1], ACT.Sqrt, bias=eps[:, :], scale=1.0 / D)\
                    .then_inc(s["x1_rooted"], 1)

            mix_high(0)
            for i in range(NT):
                if i + 1 < NT:
                    mix_high(i + 1)
                if i >= 1:
                    h2_high(i - 1)
                if i >= 1:
                    act.wait_ge(s["h2_turned"], i)
                x1_square(i)
            h2_high(NT - 1)

            def group(g, first, last):
                def load_count(m):
                    return (3 * g + m // 2 + 1) * 16

                def high(m, dst):
                    act.wait_ge(ffn_loaded[m % 2], load_count(m))
                    nc.scalar.activation(dst, raw[:, m % 2, :], ACT.Copy).then_inc(s["ffn_hi_made"], 1)

                def first_tap(m):
                    pair, up = m // 2, m % 2
                    act.wait_ge(s["up_done"], 4 * g + m + 1)
                    if not first:
                        act.wait_ge(s["act_split"], 2 * g + pair - 1)
                    c = 2 * g + pair + FT * up
                    bias = vec[:, bass.ds(c + VEC_ROWS["b_ffn"], 1)]
                    tap = vec[:, bass.ds(c + (VEC_A + VEC_B), 1)]
                    dst = (conv_g, conv_u)[up][:, pair, :]
                    nc.scalar.activation(dst, pz[up][:, :], ACT.Identity, bias=bias, scale=tap)\
                        .then_inc(s["conv_first"], 1)

                def silu_high(pair):
                    act.wait_ge(s["conv_made"], 4 * g + 2 * pair + 1)
                    nc.scalar.activation(conv_g[:, pair, :], conv_g[:, pair, :], ACT.Silu).then_inc(s["silu_made"], 1)
                    act.wait_ge(s["prod_made"], 2 * g + pair + 1)
                    if not first and pair == 0:
                        act.wait_ge(s["down_done"], 16 * g)
                    nc.scalar.activation(act_hi[:, pair, :], conv_g[:, pair, :], ACT.Copy)\
                        .then_inc(s["act_hi_made"], 1)

                act.wait_ge(s["up_done"], 4 * g + 1)
                high(2, w_hi[0][:, :])
                first_tap(0)
                act.wait_ge(s["up_done"], 4 * g + 2)
                high(3, w_hi[1][:, :])
                first_tap(1)
                silu_high(0)
                for m in range(PAIRS):
                    high(4 + m, wd_hi[:, m, :])
                if not last:
                    act.wait_ge(s["up_done"], 4 * g + 3)
                    high(6, w_hi[0][:, :])
                first_tap(2)
                if not last:
                    act.wait_ge(s["up_done"], 4 * g + 4)
                    high(7, w_hi[1][:, :])
                first_tap(3)
                silu_high(1)

            for m in range(2):
                act.wait_ge(ffn_loaded[m], 16)
                act.wait_ge(s["out_done"], 2 * (NT - 1 + m))
                nc.scalar.activation(w_hi[m][:, :], raw[:, m, :], ACT.Copy).then_inc(s["ffn_hi_made"], 1)
            group(0, True, False)
            with act.Fori(1, GROUPS - 1) as g:
                group(g, False, False)
            group(GROUPS - 1, False, True)

            for i in range(NT):
                if i:
                    act.wait_ge(s["x2_squared"], i)
                for half in range(2):
                    act.wait_ge(s["down_added"], 16 * (GROUPS - 1) + 2 * i + half + 1)
                    last = nc.scalar.activation(ysq[:, half * HALF:(half + 1) * HALF]
                                                .rearrange("p (c t) -> p c t", c=4), x1(i, half), ACT.Square,
                                                accum_out=ss3[:, i, half:half + 1])
                last.then_inc(s["x2_squared"], 1)
                act.wait_ge(s["x2_mean"], i + 1)
                nc.scalar.activation(root[:, i:i + 1], ms3[:, i:i + 1], ACT.Sqrt, bias=eps[:, :], scale=1.0 / D)\
                    .then_inc(s["x2_rooted"], 1)

        @block.vector
        def _(dve):
            steps = [0]

            def after(ins):
                steps[0] += 1
                ins.then_inc(s["dve_step"], 1)
                dve.wait_ge(s["dve_step"], steps[0])

            dve.wait_ge(s["vec_turned"], 3)
            nc.vector.tensor_copy(vec[:, 0:VEC_A], bank[4][:, 0:VEC_A])
            nc.vector.tensor_copy(vec[:, VEC_A:VEC_A + VEC_B], bank[5][:, 0:VEC_B])
            nc.vector.tensor_copy(vec[:, VEC_A + VEC_B:VECS], bank[6][:, 0:VEC_C]).then_inc(s["vec_ready"], 1)
            for i in range(NT):
                dve.wait_ge(s["x_rooted"], i + 1)
                after(nc.vector.reciprocal(rstd[:, i:i + 1], root[:, i:i + 1]))
                nc.vector.tensor_scalar(x_hat[:, i, :], x_in[:, i, :], rstd[:, i:i + 1], None, ALU.mult)\
                    .then_inc(s["x_scaled"], 1)

            def h_low(n):
                half, k = n // NK, n % NK
                dve.wait_ge(s["h_hi_made"], n + 1)
                t = slice(half * HALF, (half + 1) * HALF)
                nc.vector.scalar_tensor_tensor(out=h_lo[:, k, t], in0=bank[k], scalar=column("g1", k),
                                               in1=h_hi[:, k, t].bitcast(F32), op0=ALU.mult, op1=ALU.subtract)\
                    .then_inc(s["h_lo_made"], 1)

            def weight_low(b):
                dve.wait_ge(s["z_hi_made"], b + 1)
                nc.vector.tensor_tensor(w_lo[b % 2][:, :], raw[:, b % 2, :], w_hi[b % 2][:, :].bitcast(F32),
                                        ALU.subtract).then_inc(s["z_split"], 1)

            for n in range(NK):
                h_low(n)
            dve.wait_ge(s["gate_w_loaded"], 16)
            dve.wait_ge(s["gate_w_cleared"], 1)
            spread = raw[:, 0, :].rearrange("p (k n) -> p k n", k=NK)
            for a, c in ((0, 0), (32, ML_HEADS)):
                nc.vector.tensor_copy(spread[:, :, a:a + ML_HEADS], gate_w[:, :, c:c + ML_HEADS])\
                    .then_inc(s["gate_w_spread"], 1)
            weight_low(0)
            weight_low(1)
            for n in range(NK, 2 * NK):
                h_low(n)

            def row(ins, step):
                ins.then_inc(s["row_step"], 1)
                dve.wait_ge(s["row_step"], step)

            def gate_rows():
                a, b, c, d = (r[0:ML_HEADS, :] for r in (row_a, row_b, row_c, row_d))
                b32, c32, d32 = (r[32:36, :] for r in (row_b, row_c, row_d))
                dve.wait_ge(s["f_ln"], 1)
                row(nc.vector.scalar_tensor_tensor(out=b32, in0=b32, scalar=0.0, in1=c32, op0=ALU.min,
                                                   op1=ALU.subtract), ROW_LOGF)
                row(nc.vector.tensor_tensor_scan(d32, reset[32:36, :], b32, 0.0, ALU.mult, ALU.add), ROW_CUM)
                row(nc.vector.tensor_copy(b, d32), ROW_CUM0)
                dve.wait_ge(s["gi_ready"], 1)
                row(nc.vector.tensor_tensor(a, a, b, ALU.subtract), ROW_G)
                row(nc.vector.tensor_copy(c[:, P:S:P], b[:, P - 1:S - P:P]), ROW_RESET)
                row(nc.vector.tensor_tensor_scan(d, c, a, 0.0, ALU.add, ALU.max), ROW_MAX)
                row(nc.vector.tensor_tensor(m_prev[:, 1:NT], b[:, P - 1:S - P:P], d[:, P - 1:S - P:P], ALU.add),
                    ROW_PREV)
                row(nc.vector.tensor_tensor(c.rearrange("h (i t) -> h i t", t=P),
                                            m_prev[:, :].unsqueeze(2).to_broadcast([ML_HEADS, NT, P]),
                                            d.rearrange("h (i t) -> h i t", t=P), ALU.subtract), ROW_INTER)
                row(nc.vector.tensor_tensor(b, b, d, ALU.add), ROW_M)
                row(nc.vector.tensor_scalar(d, d, -1.0, None, ALU.mult), ROW_NEGMAX)

            def conv_qk(j):
                n = j - MQ
                dve.wait_ge(s["z_evac"], j + 2)
                if n == 0:
                    dve.wait_ge(s["row_step"], ROW_NEGMAX)
                else:
                    dve.wait_ge(s["qk_made"], n)

                def tap(t):
                    return column("w_qk", 4 * t + n)

                def done():
                    dve.wait_ge(s["qk_tap"], done.n)

                done.n = ML_TAPS * n + 1
                nc.vector.tensor_scalar(qk_acc[:, :], z[:, j, :], tap(ML_TAPS - 1), column("b_qk", n), ALU.mult,
                                        ALU.add).then_inc(s["qk_tap"], 1)
                for back in range(1, ML_TAPS):
                    done()
                    done.n += 1
                    nc.vector.scalar_tensor_tensor(out=qk_acc[:, back:], in0=z[:, j, 0:S - back],
                                                   scalar=tap(ML_TAPS - 1 - back), in1=qk_acc[:, back:],
                                                   op0=ALU.mult, op1=ALU.add).then_inc(s["qk_tap"], 1)

            def silu_qk(j):
                n = j - MQ
                dve.wait_ge(s["qk_sig_made"], n + 1)
                nc.vector.scalar_tensor_tensor(out=z[:, j, :], in0=qk_acc[:, :],
                                               scalar=ML_SCALE if j < MK else 1.0, in1=qk_sig[:, :],
                                               op0=ALU.mult, op1=ALU.mult).then_inc(s["qk_made"], 1)
                if j < MK:
                    dve.wait_ge(s["qk_made"], n + 1)
                    dve.wait_ge(s["rows_spread"], 16 * 8)
                    nc.vector.tensor_tensor(q_inter[:, n, :], q_inter[:, n, :], z[:, j, :], ALU.mult)\
                        .then_inc(s["q_inter_made"], 1)

            for b in range(ZT + 1):
                if b + 2 <= ZT:
                    weight_low(b + 2)
                if b == 0:
                    gate_rows()
                j = b - 1
                if MQ < j <= MV:
                    silu_qk(j - 1)
                if MQ <= j < MV:
                    conv_qk(j)
                if j == MV + 1:
                    dve.wait_ge(s["gates_turned"], 2)
                    dve.wait_ge(s["qk_made"], 4)
                    nc.vector.tensor_copy(carry[:, :, :], bank[5][:, 0:2 * NT].rearrange("p (r i) -> p r i", r=2))\
                        .then_inc(s["carry_ready"], 1)
                    nc.vector.tensor_copy(gates_t[:, :, :], bank[4][:, 0:NT * 36]
                                          .rearrange("p (i r) -> p i r", i=NT)).then_inc(s["gates_t_ready"], 1)
                    dve.wait_ge(s["gates_t_ready"], 1)
                    for i in range(NT):
                        for h in range(ML_HEADS):
                            d = decay[:, h, i * P:(i + 1) * P]
                            nc.vector.tensor_scalar(d, d, gates_t[:, i, h:h + 1], 0.0, ALU.add, ALU.min)\
                                .then_inc(s["decay_arg"], 1)
                    dve.wait_ge(s["small_loaded"], 48)
                    for a in range(2):
                        rows = slice(a * 64, (a + 1) * 64)
                        nc.vector.tensor_copy(sink[rows, :], sinks[rows, a:ATT_HEADS:2])
                        last = nc.vector.tensor_scalar(neg_sink[rows, :], sinks[rows, a:ATT_HEADS:2], -1.0, None,
                                                       ALU.mult)
                    after(last)

            def att_top(n):
                _, kw = keys(n)
                u = n % 2
                dve.wait_ge(s["att_scored"], n + 1)
                sc = pz[u][:, :].rearrange("p (v c) -> p v c", v=2)[:, :, 0:256]\
                    .rearrange("p v (g t) -> p v g t", g=2)[:, :, :, 0:kw]
                nc.vector.tensor_reduce(top[:, u, :].rearrange("p (v g) -> p v g", v=2), sc, AX_X, ALU.max).then_inc(s["att_topped"], 1)
                dve.wait_ge(s["att_topped"], 3 * n + 1)
                nc.vector.scalar_tensor_tensor(out=neg_top[:, u, :], in0=top[:, u, :], scalar=-ATT_SCALE,
                                               in1=neg_sink[:, :], op0=ALU.mult, op1=ALU.min)\
                    .then_inc(s["att_topped"], 1)
                dve.wait_ge(s["att_topped"], 3 * n + 2)
                nc.vector.tensor_tensor(sink_arg[:, u, :], sink[:, :], neg_top[:, u, :], ALU.add)\
                    .then_inc(s["att_topped"], 1)

            def att_sum(n):
                u = n % 2
                dve.wait_ge(s["att_exped"], n + 1)
                nc.vector.tensor_tensor(total1[:, u, :], total[:, u, :], sink_e[:, u, :], ALU.add)\
                    .then_inc(s["att_summed"], 1)
                dve.wait_ge(s["att_summed"], 3 * n + 1)
                if n >= 2:
                    dve.wait_ge(s["att_scaled"], n - 1)
                nc.vector.reciprocal(inv[:, u, :], total1[:, u, :]).then_inc(s["att_summed"], 2)

            def att_p_keep(n):
                _, kw = keys(n)
                u = n % 2
                dve.wait_ge(s["att_p_turned"], n + 1)
                if n >= 2:
                    dve.wait_ge(s["att_done"], n - 1)
                nc.vector.tensor_copy(probs_t[0:kw, u, :, :], bank[4 + u][0:kw, :].rearrange("p (j t) -> p j t", j=4))\
                    .then_inc(s["att_p_made"], 1)

            def att_keep(n):
                dve.wait_ge(s["att_done"], n + 1)
                nc.vector.tensor_copy(zq[:, n, :, :],
                                      bank[6 + n % 2][:, 0:256].rearrange("p (j d) -> p j d", j=4))\
                    .then_inc(s["att_kept"], 1)

            def wo_low(k):
                dve.wait_ge(s["wo_hi_made"], k + 1)
                gain = column("g_att", k) if k < 4 else column("g_ml", k - 4)
                nc.vector.scalar_tensor_tensor(out=wo_lo[:, k, :], in0=raw[:, (k + 1) % 2, :], scalar=gain,
                                               in1=wo_hi[:, k, :].bitcast(F32), op0=ALU.mult, op1=ALU.subtract)\
                    .then_inc(s["wo_split"], 1)

            for n in range(NC + 3):
                if n < NC:
                    att_top(n)
                if 1 <= n <= NC:
                    att_sum(n - 1)
                if 2 <= n <= NC + 1:
                    att_p_keep(n - 2)
                if n >= 3:
                    att_keep(n - 3)
                if n % 2 == 0 and 1 <= n // 2 <= NK:
                    wo_low(n // 2 - 1)

            for b in range(2):
                last = nc.vector.memset(ml_v[:, b, :, ML_V:ML_V + 1], 1.0)
            last.then_inc(s["ml_ones"], 1)

            def ml_weigh(i):
                dve.wait_ge(s["ml_scored"], i + 1)
                dve.wait_ge(s["decay_made"], i + 1)
                if i >= 2:
                    dve.wait_ge(s["ml_summed"], i - 1)
                for e in range(2):
                    last = nc.vector.tensor_tensor(ml_p[:, i % 2, e, :, :],
                                                   bank[e][:, 0:256].rearrange("p (r t) -> p r t", r=2),
                                                   decay[:, e:ML_HEADS:2, i * P:(i + 1) * P], ALU.mult)
                last.then_inc(s["ml_p_made"], 1)
                dve.wait_ge(s["ml_k_turned"], i + 1)
                if i >= 2:
                    dve.wait_ge(s["ml_stated"], i - 1)
                w = decay[:, :, (i + 1) * P - 1:(i + 1) * P].to_broadcast([P, ML_HEADS, ML_QK])
                nc.vector.tensor_tensor(ml_k[:, i % 2, :].rearrange("p (h d) -> p h d", h=ML_HEADS),
                                        bank[4][:, 0:256].rearrange("p (h d) -> p h d", h=ML_HEADS), w, ALU.mult)\
                    .then_inc(s["ml_k_made"], 1)

            def ml_carry(i):
                dve.wait_ge(s["ml_stated"], i + 1)
                if i:
                    dve.wait_ge(s["ml_state_made"], 2 * i)
                for r in range(2):
                    new = state[:, (i + 1) % 2, r, :]
                    add = bank[7][:, r * 256:r * 256 + ML_V + 1]
                    if i == 0:
                        nc.vector.tensor_copy(new, add).then_inc(s["ml_state_made"], 1)
                    else:
                        nc.vector.scalar_tensor_tensor(out=new, in0=state[:, i % 2, r, :],
                                                       scalar=carry[:, r, i:i + 1], in1=add, op0=ALU.mult,
                                                       op1=ALU.add).then_inc(s["ml_state_made"], 1)

            def ml_out(i):
                u = i % 2
                dve.wait_ge(s["ml_summed"], i + 1)
                num = pz[1][:, :].rearrange("p (e c) -> p e c", e=2)[:, :, 0:2 * (ML_V + 1)]\
                    .rearrange("p e (r c) -> p e r c", r=2)
                d4 = den[:, u, :].rearrange("p (e r) -> p e r", e=2)
                nc.vector.scalar_tensor_tensor(out=d4, in0=num[:, :, :, ML_V], scalar=-1.0,
                                               in1=gates_t[:, i, 32:36].rearrange("p (r e) -> p e r", r=2),
                                               op0=ALU.mult, op1=ALU.max).then_inc(s["ml_den"], 1)
                dve.wait_ge(s["ml_den"], 2 * i + 1)
                nc.vector.tensor_tensor(d4, num[:, :, :, ML_V], d4, ALU.max).then_inc(s["ml_den"], 1)
                dve.wait_ge(s["ml_den"], 2 * i + 2)
                nc.vector.reciprocal(inv_den[:, u, :], den[:, u, :]).then_inc(s["ml_inv"], 1)
                dve.wait_ge(s["ml_inv"], i + 1)
                for e in range(2):
                    nc.vector.tensor_tensor(ml_t[:, u, e:ML_HEADS:2, :], num[:, e, :, 0:ML_V],
                                            inv_den[:, u, 2 * e:2 * e + 2].unsqueeze(2).to_broadcast([P, 2, ML_V]),
                                            ALU.mult).then_inc(s["ml_divided"], 1)
                dve.wait_ge(s["ml_divided"], 2 * i + 2)
                dve.wait_ge(s["ml_o_turned"], i + 1)
                nc.vector.tensor_tensor(z[:, MV:MV + 4, i * P:(i + 1) * P], ml_t[:, u, :, :],
                                        bank[6].rearrange("p (h t) -> p h t", h=ML_HEADS), ALU.mult)\
                    .then_inc(s["ml_kept"], 1)

            for i in range(NT):
                ml_weigh(i)
                if i + 1 < NT:
                    ml_carry(i)
                ml_out(i)

            dve.wait_ge(s["norm_rooted"], 1)
            nc.vector.reciprocal(r_att[:, :], r_att0[:, :])
            nc.vector.reciprocal(r_ml[:, :, :].rearrange("p i h -> p (i h)"), r_ml0[:, :]).then_inc(s["norm_made"], 1)
            dve.wait_ge(s["norm_made"], 1)

            def mix_scale(i):
                for n in (2 * i, 2 * i + 1):
                    v = zq[:, n, :, :]
                    nc.vector.tensor_scalar(v, v, r_att[:, n:n + 1], None, ALU.mult)
                v = z[:, MV:MV + 4, i * P:(i + 1) * P]
                nc.vector.tensor_tensor(v, v, r_ml[:, i, :].unsqueeze(2).to_broadcast([P, ML_HEADS, P]), ALU.mult)\
                    .then_inc(s["mix_scaled"], 1)

            def mix_low(i):
                dve.wait_ge(s["mix_hi_made"], i + 1)
                nc.vector.tensor_tensor(mix_lo[i % 2][:, :, :].rearrange("p k t -> p (k t)"), pz[0][:, :],
                                        mix_hi[i % 2][:, :, :].rearrange("p k t -> p (k t)").bitcast(F32),
                                        ALU.subtract).then_inc(s["mix_lo_made"], 1)

            def add_x(i):
                dve.wait_ge(x_reloaded[i % 2], 16 * (i // 2 + 1))
                for half in range(2):
                    dve.wait_ge(s["out_done"], 2 * i + half + 1)
                    nc.vector.tensor_tensor(x1(i, half), x_again[:, i % 2, half * HALF:(half + 1) * HALF]
                                            .rearrange("p (c t) -> p c t", c=4),
                                            bank[4 + (2 * i + half) % 4].rearrange("p (c t) -> p c t", c=4), ALU.add)\
                        .then_inc(s["x1_added"], 1)
                dve.wait_ge(s["x1_squared"], i + 1)
                nc.vector.tensor_tensor(ms2[:, i:i + 1], ss2[:, i, 0:1], ss2[:, i, 1:2], ALU.add)\
                    .then_inc(s["x1_mean"], 1)
                dve.wait_ge(s["x1_rooted"], i + 1)
                after(nc.vector.reciprocal(rstd[:, i:i + 1], root[:, i:i + 1]))
                for half in range(2):
                    last = nc.vector.tensor_scalar(x_hat2[:, half * HALF:(half + 1) * HALF]
                                                   .rearrange("p (c t) -> p c t", c=4), x1(i, half),
                                                   rstd[:, i:i + 1], None, ALU.mult)
                last.then_inc(s["x1_scaled"], 1)

            def h2_low(i):
                dve.wait_ge(s["h2_turned"], i + 1)
                if i:
                    dve.wait_ge(s["h2_lo_made"], i)
                nc.vector.tensor_tensor(h2_f[:, :, :], pz[1][:, :].rearrange("p (k t) -> p k t", k=NK),
                                        column("g2", 0, NK).unsqueeze(2).to_broadcast([P, NK, P]), ALU.mult)\
                    .then_inc(s["h2_f_made"], 1)
                dve.wait_ge(s["h2_hi_made"], i + 1)
                t = slice(i * P, (i + 1) * P)
                nc.vector.tensor_tensor(h2_lo_a[:, :, t], h2_f[:, 0:6, :], h2_hi_a[:, :, t].bitcast(F32), ALU.subtract)
                nc.vector.tensor_tensor(h2_b[:, 2:4, t], h2_f[:, 6:8, :], h2_b[:, 0:2, t].bitcast(F32), ALU.subtract)\
                    .then_inc(s["h2_lo_made"], 1)

            mix_scale(0)
            mix_scale(1)
            mix_low(0)
            for i in range(NT):
                if i + 1 < NT:
                    mix_low(i + 1)
                if i + 2 < NT:
                    mix_scale(i + 2)
                if i >= 1:
                    h2_low(i - 1)
                add_x(i)
            h2_low(NT - 1)

            def group(g, first, last):
                def low(m, dst, hi):
                    dve.wait_ge(s["ffn_hi_made"], 6 * g + m + 1)
                    nc.vector.tensor_tensor(dst, raw[:, m % 2, :], hi.bitcast(F32), ALU.subtract)\
                        .then_inc(s["ffn_split"], 1)

                def taps(m):
                    pair, up = m // 2, m % 2
                    dve.wait_ge(s["conv_first"], 4 * g + m + 1)
                    c = 2 * g + pair + FT * up
                    dst = (conv_g, conv_u)[up][:, pair, :]
                    nc.vector.scalar_tensor_tensor(out=dst[:, 1:], in0=pz[up][:, 0:S - 1],
                                                   scalar=vec[:, bass.ds(c + (VEC_A + 2 * FT), 1)], in1=dst[:, 1:],
                                                   op0=ALU.mult, op1=ALU.add).then_inc(s["conv_tap"], 1)
                    dve.wait_ge(s["conv_tap"], 4 * g + m + 1)
                    nc.vector.scalar_tensor_tensor(out=dst[:, 2:], in0=pz[up][:, 0:S - 2],
                                                   scalar=vec[:, bass.ds(c + VEC_A, 1)], in1=dst[:, 2:],
                                                   op0=ALU.mult, op1=ALU.add).then_inc(s["conv_made"], 1)

                def product(pair):
                    dve.wait_ge(s["silu_made"], 2 * g + pair + 1)
                    dve.wait_ge(s["conv_made"], 4 * g + 2 * pair + 2)
                    nc.vector.tensor_tensor(conv_g[:, pair, :], conv_g[:, pair, :], conv_u[:, pair, :], ALU.mult)\
                        .then_inc(s["prod_made"], 1)

                def act_low(pair):
                    dve.wait_ge(s["act_hi_made"], 2 * g + pair + 1)
                    nc.vector.tensor_tensor(act_lo[:, pair, :], conv_g[:, pair, :], act_hi[:, pair, :].bitcast(F32),
                                            ALU.subtract).then_inc(s["act_split"], 1)

                low(2, w_lo[0][:, :], w_hi[0][:, :])
                taps(0)
                low(3, w_lo[1][:, :], w_hi[1][:, :])
                taps(1)
                if not first:
                    adds(g - 1, 0, 6)
                product(0)
                if not first:
                    adds(g - 1, 6, 16)
                act_low(0)
                for m in range(PAIRS):
                    low(4 + m, wd_lo[:, m, :], wd_hi[:, m, :])
                if not last:
                    low(6, w_lo[0][:, :], w_hi[0][:, :])
                taps(2)
                if not last:
                    low(7, w_lo[1][:, :], w_hi[1][:, :])
                taps(3)
                product(1)
                act_low(1)

            def add(g, n):
                dve.wait_ge(s["down_done"], 16 * g + n + 1)
                v = x1(n // 2, n % 2)
                nc.vector.tensor_tensor(v, v, bank[4 + n % 4].rearrange("p (c t) -> p c t", c=4), ALU.add)\
                    .then_inc(s["down_added"], 1)

            def adds(g, a, b):
                for n in range(a, b):
                    add(g, n)

            for m in range(2):
                dve.wait_ge(s["ffn_hi_made"], m + 1)
                nc.vector.tensor_tensor(w_lo[m][:, :], raw[:, m, :], w_hi[m][:, :].bitcast(F32), ALU.subtract)\
                    .then_inc(s["ffn_split"], 1)
            group(0, True, False)
            with dve.Fori(1, GROUPS - 1) as g:
                group(g, False, False)
            group(GROUPS - 1, False, True)

            dve.wait_ge(s["final_g_loaded"], 16)

            def finish(i):
                dve.wait_ge(s["x2_squared"], i + 1)
                nc.vector.tensor_tensor(ms3[:, i:i + 1], ss3[:, i, 0:1], ss3[:, i, 1:2], ALU.add)\
                    .then_inc(s["x2_mean"], 1)
                dve.wait_ge(s["x2_rooted"], i + 1)
                nc.vector.reciprocal(rstd[:, i:i + 1], root[:, i:i + 1]).then_inc(s["x2_rstd"], 1)
                dve.wait_ge(s["x2_rstd"], i + 1)
                for half in range(2):
                    c = slice(half * HALF, (half + 1) * HALF)
                    last = nc.vector.scalar_tensor_tensor(
                        out=y[i][:, c].rearrange("p (c t) -> p c t", c=4), in0=x1(i, half), scalar=rstd[:, i:i + 1],
                        in1=final_gb[:, c].rearrange("p (c t) -> p c t", c=4), op0=ALU.mult, op1=ALU.mult)
                last.then_inc(s["y_made"], 1)

            for i in range(NT):
                adds(GROUPS - 1, 2 * i, 2 * i + 2)
                if i:
                    finish(i - 1)
            finish(NT - 1)

        @block.tensor
        def _(pe):
            mm = nc.tensor.matmul

            pe.wait_ge(s["const_made"], 1)
            pe.wait_ge(s["vec_loaded"], 16 * 14)
            for n, rows in enumerate((VEC_A, VEC_B, VEC_C)):
                nc.tensor.transpose(bank[4 + n][:, 0:rows], vec_rows[0:rows, n, :], ident[0:rows, 0:rows])\
                    .then_inc(s["vec_turned"], 1)
            for half in range(2):
                for t in range(4):
                    i = 4 * half + t
                    pe.wait_ge(s["x_scaled"], i + 1)
                    for k in range(NK):
                        if i == 0 and k == 4:
                            pe.wait_ge(s["vec_ready"], 1)
                        if half and t == 0:
                            pe.wait_ge(s["h_lo_made"], k + 1)
                        ins = nc.tensor.transpose(bank[k][:, t * P:(t + 1) * P], x_hat[:, i, k * P:(k + 1) * P],
                                                  ident[:, :])
                        if t == 3:
                            ins.then_inc(s["x_turned"], 1)

            def project(dst, hi, lo, xs, halves=(0, 1)):
                for k in range(NK):
                    c = slice(k * P, (k + 1) * P)
                    xh, xl = xs(0, k), xs(1, k)
                    for w, v, first, last in ((hi, xh, k == 0, False), (hi, xl, False, False),
                                              (lo, xh, False, k == NK - 1)):
                        for h in halves:
                            ins = mm(dst[:, h * HALF:(h + 1) * HALF], w[:, c], v[:, h * HALF:(h + 1) * HALF],
                                     start=first, stop=last)
                return ins

            def h1(part, k):
                return (h_hi, h_lo)[part][:, k, :]

            pe.wait_ge(s["z_split"], 1)
            pe.wait_ge(s["h_lo_made"], 2 * NK)
            project(pz[0], w_hi[0], w_lo[0], h1).then_inc(s["z_done"], 1)

            def z_pair(b):
                for m in range(2):
                    u = 1 - m
                    pe.wait_ge(s["z_split"], b + m + 1)
                    if not (isinstance(b, int) and b == 1 and m == 0):
                        pe.wait_ge(s["z_evac"], b + m - 1)
                    project(pz[u], w_hi[u], w_lo[u], h1).then_inc(s["z_done"], 1)

            z_pair(1)
            with pe.Fori(3, 7, 2) as b:
                z_pair(b)
            pe.wait_ge(s["floor_made"], 1)
            pe.wait_ge(s["row_step"], ROW_G)
            for i in range(NT):
                ins = nc.tensor.transpose(bank[4][:, i * 36:(i + 1) * 36], row_a[0:36, i * P:(i + 1) * P],
                                          ident[0:36, 0:36])
            ins.then_inc(s["gates_turned"], 1)
            pe.wait_ge(s["inter_made"], 1)
            for r in range(2):
                ins = mm(bank[5][:, r * NT:(r + 1) * NT], pair_rows[0:ML_HEADS, r, :], row_c[0:ML_HEADS, P - 1:S:P],
                         start=True, stop=True)
            ins.then_inc(s["gates_turned"], 1)
            with pe.Fori(7, ZT, 2) as b:
                z_pair(b)

            def turn_values(c):
                if c == 0:
                    pe.wait_ge(s["z_evac"], ZT + 1)
                    pe.wait_ge(s["gates_t_ready"], 1)
                for n in range(4 * c, 4 * c + 4):
                    k0 = max(n - 1, 0) * CHUNK
                    ins = nc.tensor.transpose(bank[4 + c][:, (n % 4) * P:(n % 4 + 1) * P], z[:, AV, k0:k0 + P],
                                              ident[:, :])
                ins.then_inc(s["att_v_turned"], 1)

            def score(n):
                k0, kw = keys(n)
                if n >= 2:
                    pe.wait_ge(s["att_exped"], n - 1)
                for u in range(2):
                    for kv in range(KV_HEADS):
                        rows = slice(kv * HD, (kv + 1) * HD)
                        ins = mm(pz[n % 2][:, kv * HALF + u * P:kv * HALF + u * P + kw],
                                 zq[rows, n, 2 * u:2 * u + 2, :].rearrange("p c t -> p (c t)"),
                                 z[rows, AK, k0:k0 + kw], start=True, stop=True)
                ins.then_inc(s["att_scored"], 1)

            def turn_probs(n):
                _, kw = keys(n)
                pe.wait_ge(s["att_scaled"], n + 1)
                if n >= 2:
                    pe.wait_ge(s["att_p_made"], n - 1)
                if n == 0:
                    pe.wait_ge(s["att_v_made"], 4)
                for j in range(4):
                    ins = nc.tensor.transpose(bank[4 + n % 2][0:kw, j * P:(j + 1) * P], probs[:, n % 2, j, 0:kw],
                                              ident[:, :])
                ins.then_inc(s["att_p_turned"], 1)

            def attend(n):
                _, kw = keys(n)
                pe.wait_ge(s["att_p_made"], n + 1)
                if n >= 2:
                    pe.wait_ge(s["att_kept"], n - 1)
                for j in range(4):
                    kv = j // 2
                    ins = mm(bank[6 + n % 2][:, j * HD:(j + 1) * HD], probs_t[0:kw, n % 2, j, :],
                             att_v[0:kw, n, kv * HD:(kv + 1) * HD], start=True, stop=True)
                ins.then_inc(s["att_done"], 1)

            for c in range(4):
                turn_values(c)
            for n in range(NC + 2):
                if n < NC:
                    score(n)
                if 1 <= n <= NC:
                    turn_probs(n - 1)
                if n >= 2:
                    attend(n - 2)

            def ml_score(i):
                t = slice(i * P, (i + 1) * P)
                if i == 0:
                    pe.wait_ge(s["qk_made"], 4)
                    pe.wait_ge(s["att_exped"], NC)
                else:
                    pe.wait_ge(s["ml_p_made"], i)
                for h in range(ML_HEADS):
                    rows = slice((h % 2) * 64, (h % 2) * 64 + 64)
                    ins = mm(bank[h % 2][:, (h // 2) * P:(h // 2 + 1) * P], z[rows, MK + h // 2, t], z[rows, MQ + h // 2, t],
                             start=True, stop=True)
                ins.then_inc(s["ml_scored"], 1)
                if i == 0:
                    pe.wait_ge(s["att_kept"], NC)
                else:
                    pe.wait_ge(s["ml_k_made"], i)
                for r in range(2):
                    ins = nc.tensor.transpose(bank[4][:, r * P:(r + 1) * P], z[:, MK + r, t], ident[:, :])
                ins.then_inc(s["ml_k_turned"], 1)
                if i:
                    pe.wait_ge(s["ml_v_made"], i)
                for h in range(ML_HEADS):
                    ins = nc.tensor.transpose(bank[5][:, h * P:(h + 1) * P], z[:, MV + h, t], ident[:, :])
                ins.then_inc(s["ml_v_turned"], 1)
                if i:
                    pe.wait_ge(s["ml_kept"], i)
                for h in range(ML_HEADS):
                    ins = nc.tensor.transpose(bank[6][:, h * P:(h + 1) * P], z[:, MO + h, t], ident[:, :])
                ins.then_inc(s["ml_o_turned"], 1)

            def ml_state(i):
                pe.wait_ge(s["ml_k_made"], i + 1)
                pe.wait_ge(s["ml_v_made"], i + 1)
                if i:
                    pe.wait_ge(s["ml_state_made"], 2 * i)
                for h in range(ML_HEADS):
                    rows = slice((h % 2) * 64, (h % 2) * 64 + 64)
                    ins = mm(bank[7][rows, (h // 2) * 256:(h // 2) * 256 + ML_V + 1],
                             ml_k[:, i % 2, h * ML_QK:(h + 1) * ML_QK], ml_v[:, i % 2, h, :], start=True, stop=True)
                ins.then_inc(s["ml_stated"], 1)

            def ml_sum(i):
                pe.wait_ge(s["ml_p_made"], i + 1)
                pe.wait_ge(s["ml_v_made"], i + 1)
                if i == 0:
                    pe.wait_ge(s["att_p_made"], NC)
                else:
                    pe.wait_ge(s["ml_divided"], 2 * i)
                    pe.wait_ge(s["ml_state_made"], 2 * i)
                    pe.wait_ge(s["q_inter_made"], 2)
                for h in range(ML_HEADS):
                    rows = slice((h % 2) * 64, (h % 2) * 64 + 64)
                    c = (h % 2) * HALF + (h // 2) * (ML_V + 1)
                    dst = pz[1][:, c:c + ML_V + 1]
                    ins = mm(dst, ml_p[:, i % 2, h % 2, h // 2, :], ml_v[:, i % 2, h, :], start=True, stop=i == 0)
                    if i:
                        ins = mm(dst, q_inter[rows, h // 2, i * P:(i + 1) * P], state[rows, i % 2, h // 2, :],
                                 start=False, stop=True)
                ins.then_inc(s["ml_summed"], 1)

            for i in range(NT):
                ml_score(i)
                if i + 1 < NT:
                    ml_state(i)
                ml_sum(i)

            pe.wait_ge(s["att_squared"], NC)
            pe.wait_ge(s["ml_k_made"], NT)
            mm(bank[4][:, 0:NC], fold[:, :], sq_att[:, :], start=True, stop=True).then_inc(s["att_folded"], 1)

            def turn_mix(i):
                pe.wait_ge(s["mix_scaled"], i + 1)
                if i:
                    pe.wait_ge(s["mix_lo_made"], i)
                for n in (2 * i, 2 * i + 1):
                    for kv in range(2):
                        dst = pz[0][:, 2 * kv * P:(2 * kv + 2) * P].rearrange("p (a t) -> p a t", a=2)
                        c = (n % 2) * CHUNK
                        nc.tensor.transpose(dst[:, :, c:c + CHUNK],
                                            zq[:, n, 2 * kv:2 * kv + 2, :].rearrange("p j d -> p (j d)"), ident[:, :])
                for h in range(ML_HEADS):
                    ins = nc.tensor.transpose(pz[0][:, (4 + h) * P:(5 + h) * P], z[:, MV + h, i * P:(i + 1) * P],
                                              ident[:, :])
                ins.then_inc(s["mix_turned"], 1)

            def out_project(i):
                u = i % 2
                pe.wait_ge(s["mix_lo_made"], i + 1)
                if i == 0:
                    pe.wait_ge(s["wo_split"], NK)
                for half in range(2):
                    n = 2 * i + half
                    if n >= 4:
                        pe.wait_ge(s["x1_added"], n - 3)
                    c = slice(half * HALF, (half + 1) * HALF)
                    for k in range(NK):
                        mm(bank[4 + n % 4], mix_hi[u][:, k, :], wo_hi[:, k, c], start=k == 0, stop=False)
                        mm(bank[4 + n % 4], mix_hi[u][:, k, :], wo_lo[:, k, c], start=False, stop=False)
                        ins = mm(bank[4 + n % 4], mix_lo[u][:, k, :], wo_hi[:, k, c], start=False, stop=k == NK - 1)
                    ins.then_inc(s["out_done"], 1)

            def turn_h2(i):
                pe.wait_ge(s["x1_scaled"], i + 1)
                if i:
                    pe.wait_ge(s["h2_f_made"], i)
                for k in range(NK):
                    ins = nc.tensor.transpose(pz[1][:, k * P:(k + 1) * P], x_hat2[:, k * P:(k + 1) * P], ident[:, :])
                ins.then_inc(s["h2_turned"], 1)

            turn_mix(0)
            for i in range(NT):
                if i + 1 < NT:
                    turn_mix(i + 1)
                out_project(i)
                if i >= 1:
                    turn_h2(i - 1)
            turn_h2(NT - 1)

            def up(g, m):
                q = (0, 1, 2, 3)[m]
                pe.wait_ge(s["ffn_split"], 6 * g + q + 1)
                if not (isinstance(g, int) and g == 0 and m < 2):
                    pe.wait_ge(s["conv_made"], 4 * g + m - 1)
                u = m % 2
                project(pz[u], w_hi[u], w_lo[u], h2).then_inc(s["up_done"], 1)

            def down(g):
                pe.wait_ge(s["act_split"], 2 * g + 2)
                pe.wait_ge(s["ffn_split"], 6 * g + 6)
                for n in range(2 * NT):
                    i, c = n // 2, slice((n % 2) * HALF, (n % 2 + 1) * HALF)
                    if isinstance(g, int) and g == 0:
                        if n >= 4:
                            pe.wait_ge(s["down_added"], n - 3)
                    else:
                        pe.wait_ge(s["down_added"], 16 * g + n - 3)
                    dst = bank[4 + n % 4]
                    for k in range(PAIRS):
                        ah, al = (v[:, k, i * P:(i + 1) * P] for v in (act_hi, act_lo))
                        mm(dst, ah, wd_hi[:, k, c], start=k == 0, stop=False)
                        mm(dst, ah, wd_lo[:, k, c], start=False, stop=False)
                        ins = mm(dst, al, wd_hi[:, k, c], start=False, stop=k == PAIRS - 1)
                    ins.then_inc(s["down_done"], 1)

            pe.wait_ge(s["h2_lo_made"], NT)
            pe.wait_ge(s["x1_added"], 2 * NT)
            for m in range(4):
                up(0, m)
            up(1, 0)
            up(1, 1)
            down(0)
            up(1, 2)
            up(1, 3)
            with pe.Fori(2, GROUPS) as g:
                up(g, 0)
                up(g, 1)
                down(g - 1)
                up(g, 2)
                up(g, 3)
            down(GROUPS - 1)


_INS = ["x", "norm1_g", "w_in", "b_in", "w_qk_conv", "b_qk_conv", "attn_sinks", "g_att_out", "g_ml_out", "w_out",
        "norm2_g", "w_up", "w_ffn_conv", "b_ffn_conv", "w_down", "final_g"]
_OUT = ((1, S, D), "float32")


def kernel(**inputs):
    import numpy as _np
    import concourse.bacc as _bacc
    from concourse import mybir as _mybir
    from concourse.bass_utils import run_bass_kernel_spmd as _run

    nc = _bacc.Bacc("TRN2", target_bir_lowering=False, num_devices=1)
    arrays, args = {}, []
    for name in _INS:
        a = _np.ascontiguousarray(inputs[name])
        arrays[f"in_{name}"] = a
        args.append(nc.dram_tensor(f"in_{name}", a.shape, _mybir.dt.from_np(a.dtype), kind="ExternalInput").ap())
    out = nc.dram_tensor("out_0", _OUT[0], _mybir.dt.from_np(_np.dtype(_OUT[1])), kind="ExternalOutput").ap()
    hymba_kernel(nc, *args, out)
    r = _run(nc, [arrays], core_ids=[0])
    return r.results[0]["out_0"]
```

```python
from contextlib import ExitStack

import concourse.bass as bass
from concourse import mybir

ALU = mybir.AluOpType
ACT = mybir.ActivationFunctionType
AX_X = mybir.AxisListType.X
F32 = mybir.dt.float32
F32R = mybir.dt.float32r

P = 128
D = 1024
S = 1024
NK = D // P
NT = S // P
HALF = 512
CHUNK = 64
NC = S // CHUNK
EPS = 1e-6

ATT_HEADS = 8
KV_HEADS = 2
HD = 64
ML_HEADS = 4
ML_QK = 64
ML_V = 128
ATT_SCALE = HD ** -0.5
ML_SCALE = ML_QK ** -0.5
ML_TAPS = 4

F = 2816
FT = F // P
FFN_TAPS = 3
PAIRS = 2
GROUPS = FT // PAIRS

AQ, AK, AV, MQ, MK, MV, MO = 0, 4, 5, 6, 8, 10, 14
ZT = 18
GATES = ZT * P

VEC_ROWS = {}
_n = 0
for _name, _rows in (("g1", NK), ("b_in", ZT), ("g2", NK), ("g_att", 4), ("g_ml", ML_HEADS),
                     ("w_qk", 4 * ML_TAPS), ("b_qk", 4), ("b_ffn", 2 * FT)):
    VEC_ROWS[_name] = _n
    _n += _rows
VEC_A = _n
VEC_B = 2 * 2 * FT
VEC_C = 2 * FT
VECS = VEC_A + VEC_B + VEC_C

ROW_LOGF, ROW_CUM, ROW_CUM0, ROW_G, ROW_RESET, ROW_MAX, ROW_PREV, ROW_INTER, ROW_M, ROW_NEGMAX = range(1, 11)

SLOT = 4096
SLOTS = 51

START = [("x", 0), ("x", 1), ("x", 2), ("x", 3), ("w", 0), ("h", 0), ("h", 1), ("h", 2), ("h", 3), ("x", 4),
         ("h", 4), ("h", 5), ("h", 6), ("x", 5), ("h", 7), ("w", 1), ("x", 6), ("x", 7)]\
    + [("h", _n) for _n in range(NK, 2 * NK)]

ATT_BLOCK = 8


def att_step(block, half):
    return 2 * (block - ATT_BLOCK) + half - 1

RAW_COUNT = {}
_loads = [0, 0]
for _b in range(1, ZT + 1):
    _loads[_b % 2] += 32 if _b <= 4 else 16
    RAW_COUNT[_b] = _loads[_b % 2]
WO_COUNT = {}
_loads = [0, 0]
for _k in range(NK):
    _loads[(_k + 1) % 2] += 32 if _k < 4 else 16
    WO_COUNT[_k] = _loads[(_k + 1) % 2]


def hymba_kernel(nc, x, norm1_g, w_in, b_in, w_qk_conv, b_qk_conv, attn_sinks, g_att_out, g_ml_out,
                 w_out, norm2_g, w_up, w_ffn_conv, b_ffn_conv, w_down, final_g, out):
    x_d = x.rearrange("a s d -> (a s) d")
    out_d = out.rearrange("a s d -> (a s) d")
    w_in_d = w_in.rearrange("l (k p) n -> p (l k) n", p=P)
    w_out_d = w_out.rearrange("l k n -> (l k) n")
    w_up_d = w_up.rearrange("l (k p) n -> p (l k) n", p=P)
    w_down_d = w_down.rearrange("l (k p) n -> p (l k) n", p=P)

    negmax_d = nc.dram_tensor("negmax_rows", (ML_HEADS, S), F32, kind="Internal").ap()
    inter_d = nc.dram_tensor("inter_rows", (ML_HEADS, S), F32, kind="Internal").ap()

    with ExitStack() as ctx:
        def sb(name, shape, dt=F32):
            return ctx.enter_context(nc.sbuf_tensor(name, shape, dt))

        def sem(name):
            return ctx.enter_context(nc.semaphore(name))

        base = -(-nc.sbuf_base // 32) * 32
        sb("arena", [P, SLOTS * SLOT // 4])

        def at(slot, name, shape, dt=F32, extra=0):
            return nc.alloc_sbuf_tensor_at(name, [P, *shape], dt, offset=base + slot * SLOT + extra)

        h_hi = at(0, "h_hi", [NK, S], F32R)
        h_lo = at(8, "h_lo", [NK, S], F32R)
        wo_hi = at(0, "wo_hi", [NK, D], F32R)
        wo_lo = at(8, "wo_lo", [NK, D], F32R)
        act_hi = at(0, "act_hi", [PAIRS, S], F32R)
        act_lo = at(2, "act_lo", [PAIRS, S], F32R)
        conv_g = at(4, "conv_g", [PAIRS, S])
        conv_u = at(6, "conv_u", [PAIRS, S])
        wd_hi = at(8, "wd_hi", [PAIRS, D], F32R)
        wd_lo = at(10, "wd_lo", [PAIRS, D], F32R)

        z = at(16, "z", [ZT, S])
        zq = at(16, "zq", [NC, 4, CHUNK])
        x_in = at(16, "x_in", [NT, D])
        x_hat = at(24, "x_hat", [NT, D])
        junk0 = at(32, "junk0", [D])
        row_a = at(30, "row_a", [S])
        row_b = at(31, "row_b", [S])
        row_c = at(32, "row_c", [S])
        row_d = at(33, "row_d", [S])
        h2_hi_a = at(20, "h2_hi_a", [6, S], F32R)
        h2_b = at(30, "h2_b", [4, S], F32R)
        h2_lo_a = at(43, "h2_lo_a", [6, S], F32R)

        raw = at(34, "raw", [2, D])
        w_hi = [at(36 + 2 * s, f"w_hi{s}", [D], F32R) for s in range(2)]
        w_lo = [at(37 + 2 * s, f"w_lo{s}", [D], F32R) for s in range(2)]
        mix_hi = [at(36 + 2 * s, f"mix_hi{s}", [NK, P], F32R) for s in range(2)]
        mix_lo = [at(37 + 2 * s, f"mix_lo{s}", [NK, P], F32R) for s in range(2)]
        ml_v = at(20, "ml_v", [2, ML_HEADS, ML_V + 1], extra=1024)
        ml_k = at(21, "ml_k", [2, ML_HEADS * ML_QK], extra=1088)
        ml_p = at(39, "ml_p", [2, 2, 2, P])

        att_va = at(21, "att_va", [NT, P])
        att_vb = at(42, "att_vb", [NT - 1, P])
        probs = at(40, "probs", [2, 4, P])
        probs_t = at(41, "probs_t", [2, 4, P])
        ml_squares = at(40, "ml_squares", [ML_HEADS, P])
        att_squares = at(20, "att_squares", [4, HD])
        ml_gate = at(42, "ml_gate", [2, ML_HEADS, P])
        x_again = at(40, "x_again", [2, D])
        x_hat2 = at(42, "x_hat2", [D])

        decay = at(43, "decay", [ML_HEADS, S])
        qk_acc = at(47, "qk_acc", [2, S])
        reset = at(47, "reset", [S])
        ml_t = at(47, "ml_t", [2, ML_HEADS, P])
        gate_w = at(40, "gate_w", [NK, 2 * ML_HEADS])
        pair_rows = at(41, "pair_rows", [2, P])
        state = at(48, "state", [2, 2, ML_V + 1])
        q_inter = at(49, "q_inter", [2, S])
        h2_f = at(49, "h2_f", [NK, P])
        final_gb = at(50, "final_gb", [D])
        vec_rows = at(49, "vec_rows", [3, P])
        ysq = at(34, "ysq", [D])
        y = [at(s, f"y{n}", [D]) for n, s in enumerate([20, 21, 22, 23, 24, 25, 30, 31])]

        ident = sb("ident", [P, P])
        fold = sb("fold", [P, P])
        gates_t = sb("gates_t", [P, 2, NT, ML_HEADS])
        vec = sb("vec", [P, VECS])
        gate_b = sb("gate_b", [P, 1])
        eps = sb("eps", [P, 1])
        one = sb("one", [P, 1])
        ssq = sb("ssq", [P, NT])
        root = sb("root", [P, NT])
        rstd = sb("rstd", [P, NT])
        m_prev = sb("m_prev", [ML_HEADS, NT])
        carry = sb("carry", [P, 2, NT])
        sinks = sb("sinks", [P, ATT_HEADS])
        sink = sb("sink", [P, 4])
        neg_sink = sb("neg_sink", [P, 4])
        top = sb("top", [P, 2, 4])
        neg_top = sb("neg_top", [P, 2, 4])
        sink_arg = sb("sink_arg", [P, 2, 4])
        sink_e = sb("sink_e", [P, 2, 4])
        total = sb("total", [P, 2, 4])
        total1 = sb("total1", [P, 2, 4])
        inv = sb("inv", [P, 2, 4])
        den = sb("den", [P, 2, 4])
        inv_den = sb("inv_den", [P, 2, 4])
        sq_att = sb("sq_att", [P, NC])
        sq_ml = sb("sq_ml", [P, NT, ML_HEADS])
        att_sums = sb("att_sums", [P, NC])
        r_att0 = sb("r_att0", [P, NC])
        r_ml0 = sb("r_ml0", [P, NT, ML_HEADS])
        r_att = sb("r_att", [P, NC])
        r_ml = sb("r_ml", [P, NT, ML_HEADS])
        ss2 = sb("ss2", [P, NT, 2])
        ms2 = sb("ms2", [P, NT])
        ss3 = sb("ss3", [P, NT, 2])
        ms3 = sb("ms3", [P, NT])

        def column(name, n, k=1):
            c = VEC_ROWS[name] + n
            return vec[:, c:c + k]

        pz = [ctx.enter_context(nc.psum_tensor(f"pz{s}", [P, 2 * HALF], F32)) for s in range(2)]
        pd = [ctx.enter_context(nc.psum_tensor(f"pd{s}", [P, HALF], F32)) for s in range(4)]
        bank = [pz[0][:, 0:HALF], pz[0][:, HALF:], pz[1][:, 0:HALF], pz[1][:, HALF:]] + [p[:, :] for p in pd]

        names = """table_loaded gain_loaded gain_turned gain_ready vec_loaded vec_turned vec_ready
            small_loaded gate_w_loaded const_made mem_made
            x_squared x_rooted x_rstd x_scaled x_turned h_hi_made h_lo_made
            gate_w_cleared gate_w_spread z_hi_made z_split z_done z_evac
            gi_ready f_abs f_exp f_ln row_step inter_made floor_made rows_stored rows_spread
            gates_turned gates_t_ready decay_arg decay_exp decay_made
            qk_tap qk_made q_inter_made
            wo_hi_made wo_split
            att_scored att_topped att_exped att_summed att_scaled att_v_turned att_v_made
            att_p_turned att_p_made att_done att_kept att_squared dve_step
            ml_scored ml_k_turned ml_v_turned ml_o_turned ml_summed ml_stated
            ml_gate_made ml_v_made ml_k_made ml_p_made ml_state_made ml_den ml_inv ml_divided ml_kept ml_squared ml_ones
            att_folded att_rooted norm_rooted norm_made
            mix_scaled mix_turned mix_hi_made mix_lo_made out_done x1_added x1_squared x1_mean x1_rooted
            x1_rstd x1_scaled h2_turned h2_f_made h2_hi_made h2_lo_made
            ffn_hi_made ffn_split up_done conv_first conv_tap conv_made silu_made prod_made
            act_hi_made act_split down_done down_added final_g_loaded
            x2_squared x2_mean x2_rooted x2_rstd y_scaled y_made y2_made y_stored""".split()
        s = {n: sem(n) for n in names}
        x_loaded = [sem(f"x_loaded{i}") for i in range(NT)]
        x_reloaded = [sem(f"x_reloaded{i}") for i in range(2)]
        raw_loaded = [sem(f"raw_loaded{i}") for i in range(2)]
        wo_loaded = [sem(f"wo_loaded{i}") for i in range(2)]
        ffn_loaded = [sem(f"ffn_loaded{i}") for i in range(2)]

        block = ctx.enter_context(nc.Block())

        def x_bank(n):
            return bank[n] if n < NK else bank[(1, 3, 4, 5, 6, 7, 4, 5)[n - NK]]

        def h2_bank(i, half):
            return bank[4 + half] if i == NT - 1 else bank[half]

        def last_bank(n):
            return bank[(4 + n) % 8]

        def final_scale(i, half):
            c = slice(half * HALF, (half + 1) * HALF)
            return nc.vector.scalar_tensor_tensor(
                out=y[i][:, c].rearrange("p (c t) -> p c t", c=4), in0=x1(i, half), scalar=rstd[:, i:i + 1],
                in1=final_gb[:, c].rearrange("p (c t) -> p c t", c=4), op0=ALU.mult, op1=ALU.mult)

        def keys(n):
            return (0, CHUNK) if n == 0 else ((n - 1) * CHUNK, 2 * CHUNK)

        def x1(i, half):
            if half == 0:
                chunks = zq[:, 2 * i:2 * i + 2, :, :].rearrange("p n j d -> p (n j d)")
                return chunks.rearrange("p (c t) -> p c t", c=4)
            return z[:, MV:MV + 4, i * P:(i + 1) * P]

        def h2(part, k):
            if k < 6:
                return (h2_hi_a, h2_lo_a)[part][:, k, :]
            return h2_b[:, 2 * part + k - 6, :]

        @block.sync
        def _(sp):
            def load_x(tiles):
                for i in tiles:
                    sp.dma_start(x_in[:, i, :], x_d[i * P:(i + 1) * P, :]).then_inc(x_loaded[i], 16)

            load_x(range(NT // 2))
            for b in range(1, ZT + 1):
                j = b - 1
                if b >= 2:
                    sp.wait_ge(s["z_split"], b - 1)
                dst = raw[:, b % 2, :].rearrange("p (k n) -> p k n", k=NK)
                if j < 4:
                    for kv in range(KV_HEADS):
                        c = (j + 4 * kv) * HD
                        sp.dma_start(dst[:, :, kv * HD:(kv + 1) * HD], w_in_d[:, :, c:c + HD])\
                          .then_inc(raw_loaded[b % 2], 16)
                else:
                    sp.dma_start(dst, w_in_d[:, :, j * P:(j + 1) * P]).then_inc(raw_loaded[b % 2], 16)
                if b == 1:
                    load_x(range(NT // 2, NT))
            for k in range(NK):
                if k < 2:
                    sp.wait_ge(s["z_split"], ZT + k)
                else:
                    sp.wait_ge(s["wo_split"], k - 1)
                if k < 4:
                    kv, a = k // 2, k % 2
                    for pp in range(2):
                        r = (kv * 4 + 2 * pp + a) * HD
                        sp.dma_start(raw[pp * HD:(pp + 1) * HD, (k + 1) % 2, :], w_out_d[r:r + HD, :])\
                          .then_inc(wo_loaded[(k + 1) % 2], 16)
                else:
                    r = 512 + (k - 4) * P
                    sp.dma_start(raw[:, (k + 1) % 2, :], w_out_d[r:r + P, :]).then_inc(wo_loaded[(k + 1) % 2], 16)
            for i in range(NT):
                if i < 2:
                    sp.wait_ge(s["ml_squared"], NT)
                else:
                    sp.wait_ge(s["x1_squared"], 2 * (i - 1))
                sp.dma_start(x_again[:, i % 2, :], x_d[i * P:(i + 1) * P, :]).then_inc(x_reloaded[i % 2], 16)

            def up_tile(c):
                return w_up_d[:, :, bass.ds(c * P, P)]

            def load_up(slot, c):
                sp.dma_start(raw[:, slot, :].rearrange("p (k n) -> p k n", k=NK), up_tile(c))\
                  .then_inc(ffn_loaded[slot], 16)

            def load_group(g, last):
                sp.wait_ge(s["ffn_split"], 6 * g + 1)
                load_up(0, 2 * g + 1)
                sp.wait_ge(s["ffn_split"], 6 * g + 2)
                load_up(1, FT + 2 * g + 1)
                for m in range(PAIRS):
                    sp.wait_ge(s["ffn_split"], 6 * g + 3 + m)
                    sp.dma_start(raw[:, m, :], w_down_d[:, bass.ds(2 * g + m, 1), :]).then_inc(ffn_loaded[m], 16)
                if not last:
                    sp.wait_ge(s["ffn_split"], 6 * g + 5)
                    load_up(0, 2 * g + 2)
                    sp.wait_ge(s["ffn_split"], 6 * g + 6)
                    load_up(1, FT + 2 * g + 2)

            sp.wait_ge(s["ml_summed"], NT)
            sp.dma_start(final_gb[:, :], final_g.partition_broadcast(P)).then_inc(s["final_g_loaded"], 16)
            sp.wait_ge(s["wo_split"], NK)
            load_up(0, 0)
            load_up(1, FT)
            with sp.Fori(0, GROUPS - 1) as g:
                load_group(g, False)
            load_group(GROUPS - 1, True)
            for i in range(NT):
                if i < NT - 1:
                    if i < NT - 2:
                        sp.wait_ge(s["y_made"], i + 1)
                        sp.wait_ge(s["y2_made"], i + 1)
                    else:
                        sp.wait_ge(s["y_made"], i + 2)
                    sp.dma_start(out_d[i * P:(i + 1) * P, :], y[i][:, :]).then_inc(s["y_stored"], 16)
                else:
                    for half in range(2):
                        c = slice(half * HALF, (half + 1) * HALF)
                        sp.wait_ge(s["y_made"], NT + half + 1)
                        sp.dma_start(out_d[i * P:(i + 1) * P, c], y[i][:, c]).then_inc(s["y_stored"], 16)
            sp.wait_ge(s["y_stored"], 16 * (NT + 1))

        @block.gpsimd
        def _(pool):
            nc.gpsimd.memset(ident[:, :], 0.0).then_inc(s["mem_made"], 1)
            nc.gpsimd.memset(eps[:, :], EPS).then_inc(s["mem_made"], 1)
            nc.gpsimd.memset(one[:, :], 1.0).then_inc(s["mem_made"], 1)
            r = VEC_ROWS
            pool.dma_start(vec_rows[0:NK, 0, :], norm1_g[0, :].rearrange("(n p) -> n p", p=P))\
                .then_inc(s["gain_loaded"], 16)
            pool.dma_start(gate_w[:, :, :], w_in_d[:, :, GATES:GATES + 2 * ML_HEADS]).then_inc(s["gate_w_loaded"], 16)
            pool.wait_ge(s["mem_made"], 1)
            nc.gpsimd.affine_select(out=ident[:, :], in_=ident[:, :], compare_op=ALU.not_equal, fill=1.0,
                                    base=0, pattern=[[-1, P]], channel_multiplier=1).then_inc(s["const_made"], 1)
            nc.gpsimd.memset(raw[:, 0, :], 0.0).then_inc(s["gate_w_cleared"], 1)
            nc.gpsimd.memset(fold[:, :], 0.0).then_inc(s["mem_made"], 1)
            nc.gpsimd.memset(pair_rows[0:ML_HEADS, :, :], 1.0).then_inc(s["mem_made"], 1)
            nc.gpsimd.memset(reset[:, :], 1.0).then_inc(s["mem_made"], 1)
            nc.gpsimd.memset(m_prev[:, :], 0.0).then_inc(s["mem_made"], 1)
            for kv in range(KV_HEADS):
                pool.dma_start(vec_rows[r["b_in"]:r["b_in"] + 4, 0, kv * HD:(kv + 1) * HD],
                               b_in[0, kv * 4 * HD:(kv + 1) * 4 * HD].rearrange("(c d) -> c d", d=HD))\
                    .then_inc(s["vec_loaded"], 16)
            pool.dma_start(vec_rows[r["b_in"] + 4:r["b_in"] + ZT, 0, :],
                           b_in[0, 4 * P:ZT * P].rearrange("(n p) -> n p", p=P))\
                .then_inc(s["vec_loaded"], 16)
            for name, src in (("g2", norm2_g), ("g_ml", g_ml_out), ("b_qk", b_qk_conv),
                              ("b_ffn", b_ffn_conv)):
                rows = src.shape[1] // P
                pool.dma_start(vec_rows[r[name]:r[name] + rows, 0, :], src[0, :].rearrange("(n p) -> n p", p=P))\
                    .then_inc(s["vec_loaded"], 16)
            ga = g_att_out[0, :].rearrange("(v u a d) -> v a u d", v=2, u=2, a=2)
            for kv in range(2):
                pool.dma_start(vec_rows[r["g_att"] + 2 * kv:r["g_att"] + 2 * kv + 2, 0, :]
                               .rearrange("a (u d) -> a u d", u=2), ga[kv]).then_inc(s["vec_loaded"], 16)
            pool.dma_start(vec_rows[r["w_qk"]:r["w_qk"] + 4 * ML_TAPS, 0, :],
                           w_qk_conv[0].rearrange("t (n p) -> (t n) p", p=P)).then_inc(s["vec_loaded"], 16)
            for t in range(FFN_TAPS):
                row = t % 2 * 2 * FT
                pool.dma_start(vec_rows[row:row + 2 * FT, 1 + t // 2, :],
                               w_ffn_conv[0, t, :].rearrange("(n p) -> n p", p=P)).then_inc(s["vec_loaded"], 16)
            for a, col in ((0, 0), (32, ML_HEADS)):
                pool.dma_start(gate_b[a:a + ML_HEADS, :], b_in[0, GATES + col:GATES + col + ML_HEADS]
                               .rearrange("(n a) -> n a", a=1)).then_inc(s["small_loaded"], 16)
            pool.dma_start(sinks[:, :], attn_sinks[0, :].partition_broadcast(P)).then_inc(s["small_loaded"], 16)

            pool.wait_ge(s["mem_made"], 7)
            nc.gpsimd.memset(reset[:, 0:S:P], 0.0).then_inc(s["const_made"], 1)
            for n, off in enumerate((0, 64, -64)):
                if n:
                    pool.wait_ge(s["const_made"], 2 + n)
                nc.gpsimd.affine_select(out=fold[:, :], in_=fold[:, :], compare_op=ALU.not_equal, fill=1.0,
                                        base=off, pattern=[[-1, P]], channel_multiplier=1)\
                    .then_inc(s["const_made"], 1)
            nc.gpsimd.affine_select(out=pair_rows[0:ML_HEADS, :, :].rearrange("h r (e d) -> h r e d", e=2),
                                    in_=pair_rows[0:ML_HEADS, :, :].rearrange("h r (e d) -> h r e d", e=2),
                                    compare_op=ALU.is_equal, fill=0.0, base=0,
                                    pattern=[[-2, 2], [-1, 2], [0, 64]], channel_multiplier=1)\
                .then_inc(s["const_made"], 1)
            pool.wait_ge(s["x_turned"], 16)
            nc.gpsimd.memset(row_a[0:36, :], 0.0).then_inc(s["const_made"], 1)
            nc.gpsimd.memset(row_c[0:ML_HEADS, :], 0.0).then_inc(s["const_made"], 1)
            pool.wait_ge(s["inter_made"], 1)
            pool.dma_start(inter_d, row_c[0:ML_HEADS, :]).then_inc(s["rows_stored"], 16)
            pool.wait_ge(s["row_step"], ROW_NEGMAX)
            pool.dma_start(negmax_d, row_d[0:ML_HEADS, :]).then_inc(s["rows_stored"], 16)
            pool.wait_ge(s["rows_stored"], 32)
            for h in range(ML_HEADS):
                pool.dma_start(decay[:, h, :], negmax_d[h, :].partition_broadcast(P))\
                  .then_inc(s["rows_spread"], 16)
                pool.dma_start(q_inter[(h % 2) * 64:(h % 2) * 64 + 64, h // 2, :],
                             inter_d[h, :].partition_broadcast(64)).then_inc(s["rows_spread"], 16)
            for i in range(NT):
                pool.wait_ge(s["decay_exp"], i + 1)
                d = decay[:, :, i * P:(i + 1) * P]
                nc.gpsimd.affine_select(out=d, in_=d, compare_op=ALU.is_ge, fill=0.0, base=0,
                                        pattern=[[0, ML_HEADS], [1, P]], channel_multiplier=-1)\
                    .then_inc(s["decay_made"], 1)
            for n in range(NC):
                _, kw = keys(n)
                pool.wait_ge(s["att_summed"], 3 * n + 3)
                p = probs[:, n % 2, :, 0:kw]
                nc.gpsimd.tensor_tensor(p, p, inv[:, n % 2, :].unsqueeze(2).to_broadcast([P, 4, kw]), ALU.mult)\
                    .then_inc(s["att_scaled"], 1)
            for i in range(NT):
                pool.wait_ge(s["ml_divided"], 2 * i + 2)
                pool.wait_ge(s["ml_gate_made"], i + 1)
                nc.gpsimd.tensor_tensor(z[:, MV:MV + 4, i * P:(i + 1) * P], ml_t[:, i % 2, :, :],
                                        ml_gate[:, i % 2, :, :], ALU.mult).then_inc(s["ml_kept"], 1)
            pool.wait_ge(s["final_g_loaded"], 16)
            for i in range(NT - 2):
                pool.wait_ge(s["y_scaled"], i + 1)
                nc.gpsimd.tensor_tensor(y[i][:, HALF:], y[i][:, HALF:], final_gb[:, HALF:], ALU.mult)\
                    .then_inc(s["y2_made"], 1)

        @block.scalar
        def _(act):
            act.wait_ge(s["mem_made"], 3)
            nc.scalar.activation(root[:, 0:1], eps[:, :], ACT.Sqrt).then_inc(s["table_loaded"], 1)

            def x_square(i):
                act.wait_ge(x_loaded[i], 16)
                nc.scalar.activation(junk0[:, :], x_in[:, i, :], ACT.Square, accum_out=ssq[:, i:i + 1])\
                    .then_inc(s["x_squared"], 1)
                act.wait_ge(s["x_squared"], i + 1)
                if i == 0:
                    act.wait_ge(s["table_loaded"], 1)
                nc.scalar.activation(root[:, i:i + 1], ssq[:, i:i + 1], ACT.Sqrt, bias=eps[:, :], scale=1.0 / D)\
                    .then_inc(s["x_rooted"], 1)

            def h_high(n):
                half, k = n // NK, n % NK
                if n == 0:
                    act.wait_ge(s["gain_ready"], 1)
                act.wait_ge(s["x_turned"], n + 1)
                nc.scalar.activation(h_hi[:, k, half * HALF:(half + 1) * HALF], x_bank(n), ACT.Copy,
                                     scale=column("g1", k)).then_inc(s["h_hi_made"], 1)

            def weight_high(b):
                if b == 0:
                    act.wait_ge(s["gate_w_spread"], 2)
                else:
                    act.wait_ge(raw_loaded[b % 2], RAW_COUNT[b])
                if b >= 2:
                    act.wait_ge(s["z_done"], b - 1)
                nc.scalar.activation(w_hi[b % 2][:, :], raw[:, b % 2, :], ACT.Copy).then_inc(s["z_hi_made"], 1)

            for kind, n in START:
                {"x": x_square, "h": h_high, "w": weight_high}[kind](n)

            def z_keep(b):
                act.wait_ge(s["z_done"], b + 1)
                src = pz[b % 2]
                if b == 0:
                    act.wait_ge(s["const_made"], 8)
                    act.wait_ge(s["small_loaded"], 48)
                    nc.scalar.activation(row_a[0:ML_HEADS, :], src[0:ML_HEADS, :], ACT.Identity,
                                         bias=gate_b[0:ML_HEADS, :]).then_inc(s["gi_ready"], 1)
                    nc.scalar.activation(row_b[32:36, :], src[32:36, :], ACT.Identity,
                                         bias=gate_b[32:36, :]).then_inc(s["z_evac"], 1)
                    return
                j = b - 1
                act.wait_ge(s["vec_ready"], 1)
                if j == MO:
                    act.wait_ge(s["rows_stored"], 32)
                    act.wait_ge(s["gates_turned"], 2)
                    act.wait_ge(s["row_step"], ROW_NEGMAX)
                if j < AK:
                    nc.scalar.activation(zq[:, :, j, :], src[:, :].rearrange("p (n t) -> p n t", t=CHUNK),
                                         ACT.Identity, bias=column("b_in", j)).then_inc(s["z_evac"], 1)
                else:
                    nc.scalar.activation(z[:, j, :], src[:, :], ACT.Identity if j < MO else ACT.Sigmoid,
                                         bias=column("b_in", j)).then_inc(s["z_evac"], 1)

            def gate_logs():
                act.wait_ge(s["z_evac"], 1)
                nc.scalar.activation(row_c[32:36, :], row_b[32:36, :], ACT.Abs).then_inc(s["f_abs"], 1)
                act.wait_ge(s["f_abs"], 1)
                nc.scalar.activation(row_c[32:36, :], row_c[32:36, :], ACT.Exp, scale=-1.0).then_inc(s["f_exp"], 1)
                act.wait_ge(s["f_exp"], 1)
                nc.scalar.activation(row_c[32:36, :], row_c[32:36, :], ACT.Ln, bias=one[32:36, :])\
                    .then_inc(s["f_ln"], 1)

            def gate_exps():
                act.wait_ge(s["row_step"], ROW_INTER)
                nc.scalar.activation(row_c[0:ML_HEADS, :], row_c[0:ML_HEADS, :], ACT.Exp)\
                    .then_inc(s["inter_made"], 1)
                act.wait_ge(s["row_step"], ROW_M)
                nc.scalar.activation(row_a[32:36, :], row_b[0:ML_HEADS, :], ACT.Exp, scale=-1.0)\
                    .then_inc(s["floor_made"], 1)

            def decay_exps():
                for i in range(NT):
                    act.wait_ge(s["decay_arg"], ML_HEADS * (i + 1))
                    d = decay[:, :, i * P:(i + 1) * P]
                    nc.scalar.activation(d, d, ACT.Exp).then_inc(s["decay_exp"], 1)

            def silu_qk(n):
                act.wait_ge(s["qk_tap"], ML_TAPS * (n + 1))
                nc.scalar.activation(z[:, MQ + n, :], qk_acc[:, n % 2, :], ACT.Silu).then_inc(s["qk_made"], 1)

            def att_exps(n):
                _, kw = keys(n)
                act.wait_ge(s["att_topped"], 3 * n + 3)
                if n >= 2:
                    act.wait_ge(s["att_p_turned"], n - 1)
                for j in range(4):
                    sc = bank[4 + j // 2][:, (j % 2) * P:(j % 2) * P + kw]
                    nc.scalar.activation(probs[:, n % 2, j, 0:kw], sc, ACT.Exp,
                                         bias=neg_top[:, n % 2, j:j + 1], scale=ATT_SCALE,
                                         accum_out=total[:, n % 2, j:j + 1])
                nc.scalar.activation(sink_e[:, n % 2, :], sink_arg[:, n % 2, :], ACT.Exp).then_inc(s["att_exped"], 1)

            def att_v_keep():
                act.wait_ge(s["att_v_turned"], 1)
                for c, dst in enumerate((att_va[:, 0:4, :], att_va[:, 4:8, :], att_vb[:, 0:4, :], att_vb[:, 4:7, :])):
                    w = dst.shape[1]
                    last = nc.scalar.activation(dst, bank[4 + c][:, 0:w * P].rearrange("p (n d) -> p n d", n=w),
                                                ACT.Copy)
                last.then_inc(s["att_v_made"], 1)

            def att_square(n):
                act.wait_ge(s["att_kept"], n + 1)
                if n == 0:
                    act.wait_ge(s["att_scored"], 5)
                else:
                    act.wait_ge(s["att_squared"], n)
                nc.scalar.activation(att_squares[:, :, :], zq[:, n, :, :], ACT.Square,
                                     accum_out=sq_att[:, n:n + 1]).then_inc(s["att_squared"], 1)

            def wo_high(k):
                act.wait_ge(wo_loaded[(k + 1) % 2], WO_COUNT[k])
                gain = column("g_att", k) if k < 4 else column("g_ml", k - 4)
                nc.scalar.activation(wo_hi[:, k, :], raw[:, (k + 1) % 2, :], ACT.Copy, scale=gain)\
                    .then_inc(s["wo_hi_made"], 1)

            def ml_v_keep(i):
                act.wait_ge(s["ml_v_turned"], i + 1)
                act.wait_ge(s["ml_ones"], 1)
                if i == 0:
                    act.wait_ge(s["att_squared"], NC)
                if i >= 2:
                    act.wait_ge(s["ml_stated"], i - 1)
                    act.wait_ge(s["ml_summed"], i - 1)
                nc.scalar.activation(ml_v[:, i % 2, :, 0:ML_V], bank[5].rearrange("p (h d) -> p h d", h=ML_HEADS),
                                     ACT.Copy).then_inc(s["ml_v_made"], 1)

            for b in range(ZT + 1):
                if b + 2 <= ZT:
                    weight_high(b + 2)
                if b == ATT_BLOCK - 1:
                    att_v_keep()
                for half in range(2):
                    n = att_step(b + 1, half)
                    if half == 1 and b == ATT_BLOCK - 2:
                        decay_exps()
                    if 0 <= n < NC:
                        att_exps(n)
                    if half == 0:
                        z_keep(b)
                        if b == 1:
                            gate_logs()
                        if b == 3:
                            gate_exps()
                    if 0 <= n - 5 < NC:
                        att_square(n - 5)
                    if n == 20:
                        ml_v_keep(0)
                    if n in (7, 15):
                        for m in range(2):
                            silu_qk(n // 8 * 2 + m)

            def ml_gate_keep(i):
                act.wait_ge(s["ml_o_turned"], i + 1)
                if i == 0:
                    act.wait_ge(s["att_done"], NC)
                if i >= 2:
                    act.wait_ge(s["ml_kept"], i - 1)
                nc.scalar.activation(ml_gate[:, i % 2, :, :], bank[6].rearrange("p (h t) -> p h t", h=ML_HEADS),
                                     ACT.Copy).then_inc(s["ml_gate_made"], 1)

            def ml_square(i):
                act.wait_ge(s["ml_kept"], i + 1)
                if i:
                    act.wait_ge(s["ml_squared"], i)
                for h in range(ML_HEADS):
                    last = nc.scalar.activation(ml_squares[:, h, :], z[:, MV + h, i * P:(i + 1) * P], ACT.Square,
                                                accum_out=sq_ml[:, i, h:h + 1])
                last.then_inc(s["ml_squared"], 1)

            def ml_root(i):
                act.wait_ge(s["ml_squared"], i + 1)
                nc.scalar.activation(r_ml0[:, i, :], sq_ml[:, i, :], ACT.Sqrt, bias=eps[:, :], scale=1.0 / ML_V)\
                    .then_inc(s["norm_rooted"], 1)

            for i in range(NT):
                if i + 1 < NT:
                    ml_v_keep(i + 1)
                ml_gate_keep(i)
                if i == 0:
                    act.wait_ge(s["att_folded"], 1)
                    nc.scalar.activation(r_att0[:, :], att_sums[:, :], ACT.Sqrt, bias=eps[:, :],
                                         scale=1.0 / (ATT_HEADS * HD)).then_inc(s["att_rooted"], 1)
                if i < NT - 1:
                    wo_high(i)
                    if i >= 1:
                        ml_square(i - 1)
                        ml_root(i - 1)

            def mix_high(i):
                act.wait_ge(s["mix_turned"], i + 1)
                if i >= 2:
                    act.wait_ge(s["out_done"], 2 * (i - 1))
                nc.scalar.activation(mix_hi[i % 2][:, :, :].rearrange("p k t -> p (k t)"), pz[1][:, :], ACT.Copy)\
                    .then_inc(s["mix_hi_made"], 1)

            def h2_high(i):
                act.wait_ge(s["h2_f_made"], i + 1)
                t = slice(i * P, (i + 1) * P)
                nc.scalar.activation(h2_hi_a[:, :, t], h2_f[:, 0:6, :], ACT.Copy)
                nc.scalar.activation(h2_b[:, 0:2, t], h2_f[:, 6:8, :], ACT.Copy).then_inc(s["h2_hi_made"], 1)

            def x1_square(i, half):
                act.wait_ge(s["x1_added"], 2 * i + half + 1)
                nc.scalar.activation(x_again[:, i % 2, half * HALF:(half + 1) * HALF]
                                     .rearrange("p (c t) -> p c t", c=4), x1(i, half), ACT.Square,
                                     accum_out=ss2[:, i, half:half + 1]).then_inc(s["x1_squared"], 1)

            def x1_root(i):
                act.wait_ge(s["x1_squared"], 2 * i + 2)
                nc.scalar.activation(ms2[:, i:i + 1], ss2[:, i, 0:1], ACT.Identity, bias=eps[:, :], scale=1.0 / D)\
                    .then_inc(s["x1_mean"], 1)
                act.wait_ge(s["x1_mean"], i + 1)
                nc.scalar.activation(root[:, i:i + 1], ss2[:, i, 1:2], ACT.Sqrt, bias=ms2[:, i:i + 1], scale=1.0 / D)\
                    .then_inc(s["x1_rooted"], 1)

            def up_high(m):
                act.wait_ge(ffn_loaded[m], 16)
                act.wait_ge(s["out_done"], 2 * (NT - 1 + m))
                nc.scalar.activation(w_hi[m][:, :], raw[:, m, :], ACT.Copy).then_inc(s["ffn_hi_made"], 1)

            mix_high(0)
            wo_high(NK - 1)
            for i in (NT - 2, NT - 1):
                ml_square(i)
                ml_root(i)
            for i in range(NT):
                if i + 1 < NT:
                    mix_high(i + 1)
                x1_square(i, 0)
                if i == NT - 1:
                    up_high(0)
                if i >= 1:
                    h2_high(i - 1)
                x1_square(i, 1)
                x1_root(i)
            up_high(1)
            h2_high(NT - 1)

            def group(g, first, last):
                def load_count(m):
                    return (3 * g + m // 2 + 1) * 16

                def high(m, dst):
                    act.wait_ge(ffn_loaded[m % 2], load_count(m))
                    nc.scalar.activation(dst, raw[:, m % 2, :], ACT.Copy).then_inc(s["ffn_hi_made"], 1)

                def first_tap(m):
                    pair, up = m // 2, m % 2
                    act.wait_ge(s["up_done"], 4 * g + m + 1)
                    if not first:
                        act.wait_ge(s["act_split"], 2 * g + pair - 1)
                    c = 2 * g + pair + FT * up
                    bias = vec[:, bass.ds(c + VEC_ROWS["b_ffn"], 1)]
                    tap = vec[:, bass.ds(c + (VEC_A + VEC_B), 1)]
                    dst = (conv_g, conv_u)[up][:, pair, :]
                    nc.scalar.activation(dst, pz[up][:, :], ACT.Identity, bias=bias, scale=tap)\
                        .then_inc(s["conv_first"], 1)

                def silu_high(pair):
                    act.wait_ge(s["conv_made"], 4 * g + 2 * pair + 1)
                    nc.scalar.activation(conv_g[:, pair, :], conv_g[:, pair, :], ACT.Silu).then_inc(s["silu_made"], 1)
                    act.wait_ge(s["prod_made"], 2 * g + pair + 1)
                    if not first and pair == 0:
                        act.wait_ge(s["down_done"], 16 * g)
                    nc.scalar.activation(act_hi[:, pair, :], conv_g[:, pair, :], ACT.Copy)\
                        .then_inc(s["act_hi_made"], 1)

                act.wait_ge(s["up_done"], 4 * g + 1)
                high(2, w_hi[0][:, :])
                first_tap(0)
                act.wait_ge(s["up_done"], 4 * g + 2)
                high(3, w_hi[1][:, :])
                first_tap(1)
                silu_high(0)
                for m in range(PAIRS):
                    high(4 + m, wd_hi[:, m, :])
                if not last:
                    act.wait_ge(s["up_done"], 4 * g + 3)
                    high(6, w_hi[0][:, :])
                first_tap(2)
                if not last:
                    act.wait_ge(s["up_done"], 4 * g + 4)
                    high(7, w_hi[1][:, :])
                first_tap(3)
                silu_high(1)

            group(0, True, False)
            with act.Fori(1, GROUPS - 1) as g:
                group(g, False, False)
            group(GROUPS - 1, False, True)

            for i in range(NT):
                if i:
                    act.wait_ge(s["x2_squared"], i)
                for half in range(2):
                    act.wait_ge(s["down_added"], 16 * (GROUPS - 1) + 2 * i + half + 1)
                    last = nc.scalar.activation(ysq[:, half * HALF:(half + 1) * HALF]
                                                .rearrange("p (c t) -> p c t", c=4), x1(i, half), ACT.Square,
                                                accum_out=ss3[:, i, half:half + 1])
                last.then_inc(s["x2_squared"], 1)
                act.wait_ge(s["x2_squared"], i + 1)
                nc.scalar.activation(ms3[:, i:i + 1], ss3[:, i, 0:1], ACT.Identity, bias=eps[:, :], scale=1.0 / D)\
                    .then_inc(s["x2_mean"], 1)
                act.wait_ge(s["x2_mean"], i + 1)
                nc.scalar.activation(root[:, i:i + 1], ss3[:, i, 1:2], ACT.Sqrt, bias=ms3[:, i:i + 1], scale=1.0 / D)\
                    .then_inc(s["x2_rooted"], 1)
                if 0 <= i - 1 < NT - 2:
                    act.wait_ge(s["x2_rstd"], i)
                    nc.scalar.activation(y[i - 1][:, HALF:].rearrange("p (c t) -> p c t", c=4), x1(i - 1, 1), ACT.Copy,
                                         scale=rstd[:, i - 1:i]).then_inc(s["y_scaled"], 1)

        @block.vector
        def _(dve):
            steps = [0]

            def after(ins):
                steps[0] += 1
                ins.then_inc(s["dve_step"], 1)
                dve.wait_ge(s["dve_step"], steps[0])

            dve.wait_ge(s["gain_turned"], 1)
            nc.vector.tensor_copy(vec[:, 0:NK], bank[7][:, 0:NK]).then_inc(s["gain_ready"], 1)
            def spread_gates():
                dve.wait_ge(s["gate_w_loaded"], 16)
                dve.wait_ge(s["gate_w_cleared"], 1)
                spread = raw[:, 0, :].rearrange("p (k n) -> p k n", k=NK)
                for a, c in ((0, 0), (32, ML_HEADS)):
                    nc.vector.tensor_copy(spread[:, :, a:a + ML_HEADS], gate_w[:, :, c:c + ML_HEADS])\
                        .then_inc(s["gate_w_spread"], 1)

            def x_scale(i):
                dve.wait_ge(s["x_rooted"], i + 1)
                nc.vector.reciprocal(rstd[:, i:i + 1], root[:, i:i + 1]).then_inc(s["x_rstd"], 1)
                dve.wait_ge(s["x_rstd"], i + 1)
                nc.vector.tensor_scalar(x_hat[:, i, :], x_in[:, i, :], rstd[:, i:i + 1], None, ALU.mult)\
                    .then_inc(s["x_scaled"], 1)

            def h_low(n):
                half, k = n // NK, n % NK
                dve.wait_ge(s["h_hi_made"], n + 1)
                t = slice(half * HALF, (half + 1) * HALF)
                nc.vector.scalar_tensor_tensor(out=h_lo[:, k, t], in0=x_bank(n), scalar=column("g1", k),
                                               in1=h_hi[:, k, t].bitcast(F32), op0=ALU.mult, op1=ALU.subtract)\
                    .then_inc(s["h_lo_made"], 1)

            def weight_low(b):
                dve.wait_ge(s["z_hi_made"], b + 1)
                nc.vector.tensor_tensor(w_lo[b % 2][:, :], raw[:, b % 2, :], w_hi[b % 2][:, :].bitcast(F32),
                                        ALU.subtract).then_inc(s["z_split"], 1)

            for kind, n in START:
                if kind == "w" and n == 0:
                    spread_gates()
                {"x": x_scale, "h": h_low, "w": weight_low}[kind](n)

            def vectors():
                dve.wait_ge(s["vec_turned"], 3)
                nc.vector.tensor_copy(vec[:, NK:VEC_A], bank[4][:, NK:VEC_A])
                nc.vector.tensor_copy(vec[:, VEC_A:VEC_A + VEC_B], bank[5][:, 0:VEC_B])
                nc.vector.tensor_copy(vec[:, VEC_A + VEC_B:VECS], bank[6][:, 0:VEC_C]).then_inc(s["vec_ready"], 1)

            def row(ins, step):
                ins.then_inc(s["row_step"], 1)
                dve.wait_ge(s["row_step"], step)

            def gate_rows(part):
                a, b, c, d = (r[0:ML_HEADS, :] for r in (row_a, row_b, row_c, row_d))
                b32, c32, d32 = (r[32:36, :] for r in (row_b, row_c, row_d))
                if part == 0:
                    gate_sums(a, b, c, b32, c32, d32)
                else:
                    gate_maxima(a, b, c, d)

            def gate_sums(a, b, c, b32, c32, d32):
                dve.wait_ge(s["f_ln"], 1)
                row(nc.vector.scalar_tensor_tensor(out=b32, in0=b32, scalar=0.0, in1=c32, op0=ALU.min,
                                                   op1=ALU.subtract), ROW_LOGF)
                row(nc.vector.tensor_tensor_scan(d32, reset[32:36, :], b32, 0.0, ALU.mult, ALU.add), ROW_CUM)
                row(nc.vector.tensor_copy(b, d32), ROW_CUM0)
                dve.wait_ge(s["gi_ready"], 1)
                row(nc.vector.tensor_tensor(a, a, b, ALU.subtract), ROW_G)
                row(nc.vector.tensor_copy(c[:, P:S:P], b[:, P - 1:S - P:P]), ROW_RESET)

            def gate_maxima(a, b, c, d):
                row(nc.vector.tensor_tensor_scan(d, c, a, 0.0, ALU.add, ALU.max), ROW_MAX)
                row(nc.vector.tensor_tensor(m_prev[:, 1:NT], b[:, P - 1:S - P:P], d[:, P - 1:S - P:P], ALU.add),
                    ROW_PREV)
                row(nc.vector.tensor_tensor(c.rearrange("h (i t) -> h i t", t=P),
                                            m_prev[:, :].unsqueeze(2).to_broadcast([ML_HEADS, NT, P]),
                                            d.rearrange("h (i t) -> h i t", t=P), ALU.subtract), ROW_INTER)
                row(nc.vector.tensor_tensor(b, b, d, ALU.add), ROW_M)
                row(nc.vector.tensor_scalar(d, d, -1.0, None, ALU.mult), ROW_NEGMAX)

            def conv_tap(m):
                n, back = m // ML_TAPS, m % ML_TAPS
                j = MQ + n
                w = column("w_qk", 4 * (ML_TAPS - 1 - back) + n)
                if back == 0:
                    dve.wait_ge(s["z_evac"], j + 2)
                    if n >= 2:
                        dve.wait_ge(s["qk_made"], n - 1)
                    nc.vector.tensor_scalar(qk_acc[:, n % 2, :], z[:, j, :], w, column("b_qk", n), ALU.mult,
                                            ALU.add).then_inc(s["qk_tap"], 1)
                else:
                    dve.wait_ge(s["qk_tap"], m)
                    nc.vector.scalar_tensor_tensor(out=qk_acc[:, n % 2, back:], in0=z[:, j, 0:S - back], scalar=w,
                                                   in1=qk_acc[:, n % 2, back:], op0=ALU.mult, op1=ALU.add)\
                        .then_inc(s["qk_tap"], 1)

            def scale_q(n):
                dve.wait_ge(s["qk_made"], n + 1)
                dve.wait_ge(s["rows_spread"], 16 * 8)
                nc.vector.scalar_tensor_tensor(out=q_inter[:, n, :], in0=q_inter[:, n, :], scalar=ML_SCALE,
                                               in1=z[:, MQ + n, :], op0=ALU.mult, op1=ALU.mult)\
                    .then_inc(s["q_inter_made"], 1)

            def decay_args():
                dve.wait_ge(s["gates_turned"], 2)
                dve.wait_ge(s["rows_spread"], 16 * 8)
                nc.vector.tensor_copy(carry[:, :, :], bank[5][:, 0:2 * NT].rearrange("p (r i) -> p r i", r=2))
                turned = bank[4][:, 0:NT * 36].rearrange("p (i r) -> p i r", i=NT)
                for n in range(2):
                    last = nc.vector.tensor_copy(gates_t[:, n, :, :], turned[:, :, 32 * n:32 * n + ML_HEADS])
                last.then_inc(s["gates_t_ready"], 1)
                dve.wait_ge(s["gates_t_ready"], 1)
                for i in range(NT):
                    for h in range(ML_HEADS):
                        d = decay[:, h, i * P:(i + 1) * P]
                        nc.vector.tensor_scalar(d, d, gates_t[:, 0, i, h:h + 1], 0.0, ALU.add, ALU.min)\
                            .then_inc(s["decay_arg"], 1)
                dve.wait_ge(s["small_loaded"], 48)
                for a in range(2):
                    rows = slice(a * 64, (a + 1) * 64)
                    nc.vector.tensor_copy(sink[rows, :], sinks[rows, a:ATT_HEADS:2])
                    last = nc.vector.tensor_scalar(neg_sink[rows, :], sinks[rows, a:ATT_HEADS:2], -1.0, None,
                                                   ALU.mult)
                after(last)

            def att_top(n):
                _, kw = keys(n)
                u = n % 2
                dve.wait_ge(s["att_scored"], n + 1)
                for kv in range(KV_HEADS):
                    sc = bank[4 + kv][:, 0:256].rearrange("p (g t) -> p g t", g=2)[:, :, 0:kw]
                    last = nc.vector.tensor_reduce(top[:, u, 2 * kv:2 * kv + 2], sc, AX_X, ALU.max)
                last.then_inc(s["att_topped"], 1)
                dve.wait_ge(s["att_topped"], 3 * n + 1)
                nc.vector.scalar_tensor_tensor(out=neg_top[:, u, :], in0=top[:, u, :], scalar=-ATT_SCALE,
                                               in1=neg_sink[:, :], op0=ALU.mult, op1=ALU.min)\
                    .then_inc(s["att_topped"], 1)
                dve.wait_ge(s["att_topped"], 3 * n + 2)
                nc.vector.tensor_tensor(sink_arg[:, u, :], sink[:, :], neg_top[:, u, :], ALU.add)\
                    .then_inc(s["att_topped"], 1)

            def att_sum(n):
                u = n % 2
                dve.wait_ge(s["att_exped"], n + 1)
                nc.vector.tensor_tensor(total1[:, u, :], total[:, u, :], sink_e[:, u, :], ALU.add)\
                    .then_inc(s["att_summed"], 1)
                dve.wait_ge(s["att_summed"], 3 * n + 1)
                if n >= 2:
                    dve.wait_ge(s["att_scaled"], n - 1)
                nc.vector.reciprocal(inv[:, u, :], total1[:, u, :]).then_inc(s["att_summed"], 2)

            def att_p_keep(n):
                _, kw = keys(n)
                u = n % 2
                dve.wait_ge(s["att_p_turned"], n + 1)
                if n >= 2:
                    dve.wait_ge(s["att_done"], n - 1)
                nc.vector.tensor_copy(probs_t[0:kw, u, :, :], bank[6][0:kw, :].rearrange("p (j t) -> p j t", j=4))\
                    .then_inc(s["att_p_made"], 1)

            def att_keep(n):
                dve.wait_ge(s["att_done"], n + 1)
                nc.vector.tensor_copy(zq[:, n, :, :],
                                      bank[7][:, 0:256].rearrange("p (j d) -> p j d", j=4))\
                    .then_inc(s["att_kept"], 1)

            def wo_low(k):
                dve.wait_ge(s["wo_hi_made"], k + 1)
                gain = column("g_att", k) if k < 4 else column("g_ml", k - 4)
                nc.vector.scalar_tensor_tensor(out=wo_lo[:, k, :], in0=raw[:, (k + 1) % 2, :], scalar=gain,
                                               in1=wo_hi[:, k, :].bitcast(F32), op0=ALU.mult, op1=ALU.subtract)\
                    .then_inc(s["wo_split"], 1)

            def ml_ones():
                dve.wait_ge(s["att_done"], NC)
                for b in range(2):
                    last = nc.vector.memset(ml_v[:, b, :, ML_V:ML_V + 1], 1.0)
                last.then_inc(s["ml_ones"], 1)

            def ml_weigh(i):
                dve.wait_ge(s["ml_scored"], i + 1)
                dve.wait_ge(s["decay_made"], i + 1)
                if i >= 2:
                    dve.wait_ge(s["ml_summed"], i - 1)
                for e in range(2):
                    last = nc.vector.scalar_tensor_tensor(
                        out=ml_p[:, i % 2, e, :, :], in0=bank[2 + e][:, 0:256].rearrange("p (r t) -> p r t", r=2),
                        scalar=ML_SCALE, in1=decay[:, e:ML_HEADS:2, i * P:(i + 1) * P], op0=ALU.mult, op1=ALU.mult)
                last.then_inc(s["ml_p_made"], 1)
                dve.wait_ge(s["ml_k_turned"], i + 1)
                if i >= 2:
                    dve.wait_ge(s["ml_stated"], i - 1)
                w = decay[:, :, (i + 1) * P - 1:(i + 1) * P].to_broadcast([P, ML_HEADS, ML_QK])
                nc.vector.tensor_tensor(ml_k[:, i % 2, :].rearrange("p (h d) -> p h d", h=ML_HEADS),
                                        bank[4][:, 0:256].rearrange("p (h d) -> p h d", h=ML_HEADS), w, ALU.mult)\
                    .then_inc(s["ml_k_made"], 1)

            for b in range(ZT + 1):
                for half in range(2):
                    n = att_step(b + 1, half)
                    if 0 <= n < NC:
                        att_top(n)
                    if half == 0 and b + 2 <= ZT:
                        weight_low(b + 2)
                    if half == 0 and b == 0:
                        vectors()
                    if 0 <= n - 2 < NC:
                        att_p_keep(n - 2)
                    if 0 <= n - 3 < NC:
                        att_keep(n - 3)
                    if half == 0 and b in (1, 2):
                        gate_rows(b - 1)
                    if half == 1 and b == ATT_BLOCK - 2:
                        decay_args()
                    if 0 <= n < NC:
                        att_sum(n)
                    if 0 <= n < 4 * ML_TAPS:
                        conv_tap(n)
                    if n in (8, 10):
                        scale_q((n - 8) // 2)
                    if n == 19:
                        ml_ones()
                    if n == 20:
                        ml_weigh(0)

            def ml_carry(i):
                dve.wait_ge(s["ml_stated"], i + 1)
                if i == 0:
                    nc.vector.tensor_copy(att_sums[:, :], bank[7][:, HALF - NC:]).then_inc(s["att_folded"], 1)
                if i:
                    dve.wait_ge(s["ml_state_made"], 2 * i)
                    dve.wait_ge(s["ml_summed"], i)
                for r in range(2):
                    new = state[:, (i + 1) % 2, r, :]
                    add = bank[7][:, r * 256:r * 256 + ML_V + 1]
                    if i == 0:
                        nc.vector.tensor_copy(new, add).then_inc(s["ml_state_made"], 1)
                    else:
                        nc.vector.scalar_tensor_tensor(out=new, in0=state[:, i % 2, r, :],
                                                       scalar=carry[:, r, i:i + 1], in1=add, op0=ALU.mult,
                                                       op1=ALU.add).then_inc(s["ml_state_made"], 1)

            def ml_out(i):
                u = i % 2
                dve.wait_ge(s["ml_summed"], i + 1)
                num = pz[0][:, :].rearrange("p (e c) -> p e c", e=2)[:, :, 0:2 * (ML_V + 1)]\
                    .rearrange("p e (r c) -> p e r c", r=2)
                d4 = den[:, u, :].rearrange("p (e r) -> p e r", e=2)
                nc.vector.scalar_tensor_tensor(out=d4, in0=num[:, :, :, ML_V], scalar=-1.0,
                                               in1=gates_t[:, 1, i, :].rearrange("p (r e) -> p e r", r=2),
                                               op0=ALU.mult, op1=ALU.max).then_inc(s["ml_den"], 1)
                dve.wait_ge(s["ml_den"], 2 * i + 1)
                nc.vector.tensor_tensor(d4, num[:, :, :, ML_V], d4, ALU.max).then_inc(s["ml_den"], 1)
                dve.wait_ge(s["ml_den"], 2 * i + 2)
                nc.vector.reciprocal(inv_den[:, u, :], den[:, u, :]).then_inc(s["ml_inv"], 1)
                dve.wait_ge(s["ml_inv"], i + 1)
                if i >= 2:
                    dve.wait_ge(s["ml_kept"], i - 1)
                for e in range(2):
                    nc.vector.tensor_tensor(ml_t[:, u, e:ML_HEADS:2, :], num[:, e, :, 0:ML_V],
                                            inv_den[:, u, 2 * e:2 * e + 2].unsqueeze(2).to_broadcast([P, 2, ML_V]),
                                            ALU.mult).then_inc(s["ml_divided"], 1)

            def mix_scale(i):
                if i == 0:
                    dve.wait_ge(s["att_rooted"], 1)
                    nc.vector.reciprocal(r_att[:, :], r_att0[:, :])
                dve.wait_ge(s["norm_rooted"], i + 1)
                nc.vector.reciprocal(r_ml[:, i, :], r_ml0[:, i, :]).then_inc(s["norm_made"], 1)
                dve.wait_ge(s["norm_made"], i + 1)
                for n in (2 * i, 2 * i + 1):
                    v = zq[:, n, :, :]
                    nc.vector.tensor_scalar(v, v, r_att[:, n:n + 1], None, ALU.mult)
                v = z[:, MV:MV + 4, i * P:(i + 1) * P]
                nc.vector.tensor_tensor(v, v, r_ml[:, i, :].unsqueeze(2).to_broadcast([P, ML_HEADS, P]), ALU.mult)\
                    .then_inc(s["mix_scaled"], 1)

            def mix_low(i):
                dve.wait_ge(s["mix_hi_made"], i + 1)
                nc.vector.tensor_tensor(mix_lo[i % 2][:, :, :].rearrange("p k t -> p (k t)"), pz[1][:, :],
                                        mix_hi[i % 2][:, :, :].rearrange("p k t -> p (k t)").bitcast(F32),
                                        ALU.subtract).then_inc(s["mix_lo_made"], 1)

            def add_x(i, half):
                if half == 0:
                    dve.wait_ge(x_reloaded[i % 2], 16 * (i // 2 + 1))
                dve.wait_ge(s["out_done"], 2 * i + half + 1)
                nc.vector.tensor_tensor(x1(i, half), x_again[:, i % 2, half * HALF:(half + 1) * HALF]
                                        .rearrange("p (c t) -> p c t", c=4),
                                        bank[4 + (2 * i + half) % 4].rearrange("p (c t) -> p c t", c=4), ALU.add)\
                    .then_inc(s["x1_added"], 1)

            def x1_scale(i):
                dve.wait_ge(s["x1_rooted"], i + 1)
                nc.vector.reciprocal(rstd[:, i:i + 1], root[:, i:i + 1]).then_inc(s["x1_rstd"], 1)
                dve.wait_ge(s["x1_rstd"], i + 1)
                if i:
                    dve.wait_ge(s["h2_turned"], i)
                for half in range(2):
                    last = nc.vector.tensor_scalar(x_hat2[:, half * HALF:(half + 1) * HALF]
                                                   .rearrange("p (c t) -> p c t", c=4), x1(i, half),
                                                   rstd[:, i:i + 1], None, ALU.mult)
                last.then_inc(s["x1_scaled"], 1)

            def h2_low(i):
                dve.wait_ge(s["h2_turned"], i + 1)
                if i:
                    dve.wait_ge(s["h2_lo_made"], i)
                for half in range(2):
                    k = slice(half * 4, half * 4 + 4)
                    last = nc.vector.tensor_tensor(h2_f[:, k, :], h2_bank(i, half).rearrange("p (k t) -> p k t", k=4),
                                                   column("g2", half * 4, 4).unsqueeze(2).to_broadcast([P, 4, P]),
                                                   ALU.mult)
                last.then_inc(s["h2_f_made"], 1)
                dve.wait_ge(s["h2_hi_made"], i + 1)
                t = slice(i * P, (i + 1) * P)
                nc.vector.tensor_tensor(h2_lo_a[:, :, t], h2_f[:, 0:6, :], h2_hi_a[:, :, t].bitcast(F32), ALU.subtract)
                nc.vector.tensor_tensor(h2_b[:, 2:4, t], h2_f[:, 6:8, :], h2_b[:, 0:2, t].bitcast(F32), ALU.subtract)\
                    .then_inc(s["h2_lo_made"], 1)

            def up_low(m):
                dve.wait_ge(s["ffn_hi_made"], m + 1)
                nc.vector.tensor_tensor(w_lo[m][:, :], raw[:, m, :], w_hi[m][:, :].bitcast(F32), ALU.subtract)\
                    .then_inc(s["ffn_split"], 1)

            ml_carry(0)
            for i in range(NT):
                if i + 1 < NT:
                    ml_weigh(i + 1)
                if i == NT - 1:
                    mix_low(0)
                ml_out(i)
                wo_low(i)
                if i + 2 < NT:
                    ml_carry(i + 1)
                if i in (NT - 4, NT - 3):
                    mix_scale(i - NT + 4)

            for i in range(NT):
                if i + 1 < NT:
                    mix_low(i + 1)
                if i + 2 < NT:
                    mix_scale(i + 2)
                add_x(i, 0)
                if i == NT - 1:
                    up_low(0)
                if i >= 1:
                    h2_low(i - 1)
                add_x(i, 1)
                x1_scale(i)
            up_low(1)
            h2_low(NT - 1)

            def group(g, first, last):
                def low(m, dst, hi):
                    dve.wait_ge(s["ffn_hi_made"], 6 * g + m + 1)
                    nc.vector.tensor_tensor(dst, raw[:, m % 2, :], hi.bitcast(F32), ALU.subtract)\
                        .then_inc(s["ffn_split"], 1)

                def taps(m):
                    pair, up = m // 2, m % 2
                    dve.wait_ge(s["conv_first"], 4 * g + m + 1)
                    c = 2 * g + pair + FT * up
                    dst = (conv_g, conv_u)[up][:, pair, :]
                    nc.vector.scalar_tensor_tensor(out=dst[:, 1:], in0=pz[up][:, 0:S - 1],
                                                   scalar=vec[:, bass.ds(c + (VEC_A + 2 * FT), 1)], in1=dst[:, 1:],
                                                   op0=ALU.mult, op1=ALU.add).then_inc(s["conv_tap"], 1)
                    dve.wait_ge(s["conv_tap"], 4 * g + m + 1)
                    nc.vector.scalar_tensor_tensor(out=dst[:, 2:], in0=pz[up][:, 0:S - 2],
                                                   scalar=vec[:, bass.ds(c + VEC_A, 1)], in1=dst[:, 2:],
                                                   op0=ALU.mult, op1=ALU.add).then_inc(s["conv_made"], 1)

                def product(pair):
                    dve.wait_ge(s["silu_made"], 2 * g + pair + 1)
                    dve.wait_ge(s["conv_made"], 4 * g + 2 * pair + 2)
                    nc.vector.tensor_tensor(conv_g[:, pair, :], conv_g[:, pair, :], conv_u[:, pair, :], ALU.mult)\
                        .then_inc(s["prod_made"], 1)

                def act_low(pair):
                    dve.wait_ge(s["act_hi_made"], 2 * g + pair + 1)
                    nc.vector.tensor_tensor(act_lo[:, pair, :], conv_g[:, pair, :], act_hi[:, pair, :].bitcast(F32),
                                            ALU.subtract).then_inc(s["act_split"], 1)

                low(2, w_lo[0][:, :], w_hi[0][:, :])
                taps(0)
                low(3, w_lo[1][:, :], w_hi[1][:, :])
                if not first:
                    adds(g - 1, 0, 1)
                taps(1)
                if not first:
                    adds(g - 1, 1, 6)
                product(0)
                if not first:
                    adds(g - 1, 6, 16)
                act_low(0)
                for m in range(PAIRS):
                    low(4 + m, wd_lo[:, m, :], wd_hi[:, m, :])
                if not last:
                    low(6, w_lo[0][:, :], w_hi[0][:, :])
                taps(2)
                if not last:
                    low(7, w_lo[1][:, :], w_hi[1][:, :])
                taps(3)
                product(1)
                act_low(1)

            def add(g, n):
                dve.wait_ge(s["down_done"], 16 * g + n + 1)
                v = x1(n // 2, n % 2)
                src = last_bank(n) if isinstance(g, int) and g == GROUPS - 1 else bank[4 + n % 4]
                nc.vector.tensor_tensor(v, v, src.rearrange("p (c t) -> p c t", c=4), ALU.add)\
                    .then_inc(s["down_added"], 1)

            def adds(g, a, b):
                for n in range(a, b):
                    add(g, n)

            group(0, True, False)
            with dve.Fori(1, GROUPS - 1) as g:
                group(g, False, False)
            group(GROUPS - 1, False, True)

            dve.wait_ge(s["final_g_loaded"], 16)

            def finish(i):
                dve.wait_ge(s["x2_rooted"], i + 1)
                nc.vector.reciprocal(rstd[:, i:i + 1], root[:, i:i + 1]).then_inc(s["x2_rstd"], 1)
                dve.wait_ge(s["x2_rstd"], i + 1)
                final_scale(i, 0).then_inc(s["y_made"], 1)
                if i >= NT - 2:
                    final_scale(i, 1).then_inc(s["y_made"], 1)

            for i in range(NT):
                adds(GROUPS - 1, 2 * i, 2 * i + 2)
                if i:
                    finish(i - 1)
            finish(NT - 1)

        @block.tensor
        def _(pe):
            mm = nc.tensor.matmul

            pe.wait_ge(s["const_made"], 1)
            pe.wait_ge(s["gain_loaded"], 16)
            nc.tensor.transpose(bank[7][:, 0:NK], vec_rows[0:NK, 0, :], ident[0:NK, 0:NK]).then_inc(s["gain_turned"], 1)
            def turn_x(i, features):
                pe.wait_ge(s["x_scaled"], i + 1)
                for k in features:
                    if i == 0 and k == NK - 1:
                        pe.wait_ge(s["gain_ready"], 1)
                    if i == NT // 2 and k >= 6:
                        pe.wait_ge(s["h_lo_made"], NK + k - 3)
                    ins = nc.tensor.transpose(x_bank(i // 4 * NK + k)[:, i % 4 * P:(i % 4 + 1) * P],
                                              x_hat[:, i, k * P:(k + 1) * P], ident[:, :])
                    if i % 4 == 3:
                        ins.then_inc(s["x_turned"], 1)

            for i in range(NT // 2):
                turn_x(i, range(NK))

            def project(dst, hi, lo, xs, halves=(0, 1), beside=None, parts_made=None):
                for k in range(NK):
                    if parts_made is not None:
                        pe.wait_ge(s["h_lo_made"], parts_made + k + 1)
                    if beside and k % (NK // 2) == 0:
                        beside(k // (NK // 2))
                    c = slice(k * P, (k + 1) * P)
                    xh, xl = xs(0, k), xs(1, k)
                    for w, v, first, last in ((hi, xh, k == 0, False), (hi, xl, False, False),
                                              (lo, xh, False, k == NK - 1)):
                        for h in halves:
                            ins = mm(dst[:, h * HALF:(h + 1) * HALF], w[:, c], v[:, h * HALF:(h + 1) * HALF],
                                     start=first, stop=last)
                return ins

            def h1(part, k):
                return (h_hi, h_lo)[part][:, k, :]

            def turn_second(features):
                def beside(n):
                    for i in (4 + 2 * n, 5 + 2 * n):
                        turn_x(i, features)
                return beside

            def turn_rest(n):
                if n == 1:
                    for i in range(4, NT):
                        turn_x(i, (6, 7))

            pe.wait_ge(s["z_split"], 1)
            project(pz[0], w_hi[0], w_lo[0], h1, (0,), parts_made=0)
            pe.wait_ge(s["z_split"], 2)
            project(pz[1], w_hi[1], w_lo[1], h1, (0,), beside=turn_second(range(6)))
            project(pz[0], w_hi[0], w_lo[0], h1, (1,), beside=turn_rest, parts_made=NK).then_inc(s["z_done"], 1)
            pe.wait_ge(s["h_lo_made"], 2 * NK)
            pe.wait_ge(s["vec_loaded"], 16 * 13)
            for n, rows in enumerate((VEC_A, VEC_B, VEC_C)):
                nc.tensor.transpose(bank[4 + n][:, 0:rows], vec_rows[0:rows, n, :], ident[0:rows, 0:rows])\
                    .then_inc(s["vec_turned"], 1)
            project(pz[1], w_hi[1], w_lo[1], h1, (1,)).then_inc(s["z_done"], 1)

            def z_block(b, beside=None):
                pe.wait_ge(s["z_split"], b + 1)
                pe.wait_ge(s["z_evac"], b - 1)
                project(pz[b % 2], w_hi[b % 2], w_lo[b % 2], h1, beside=beside).then_inc(s["z_done"], 1)

            def z_pair(b):
                for m in range(2):
                    u = 1 - m
                    pe.wait_ge(s["z_split"], b + m + 1)
                    pe.wait_ge(s["z_evac"], b + m - 1)
                    project(pz[u], w_hi[u], w_lo[u], h1).then_inc(s["z_done"], 1)

            z_block(2)
            with pe.Fori(3, 7, 2) as b:
                z_pair(b)
            pe.wait_ge(s["floor_made"], 1)
            pe.wait_ge(s["row_step"], ROW_G)
            for i in range(NT):
                ins = nc.tensor.transpose(bank[4][:, i * 36:(i + 1) * 36], row_a[0:36, i * P:(i + 1) * P],
                                          ident[0:36, 0:36])
            ins.then_inc(s["gates_turned"], 1)
            pe.wait_ge(s["inter_made"], 1)
            for r in range(2):
                ins = mm(bank[5][:, r * NT:(r + 1) * NT], pair_rows[0:ML_HEADS, r, :], row_c[0:ML_HEADS, P - 1:S:P],
                         start=True, stop=True)
            ins.then_inc(s["gates_turned"], 1)
            z_block(7)

            def turn_values():
                pe.wait_ge(s["z_evac"], AV + 2)
                pe.wait_ge(s["gates_t_ready"], 1)
                for n in range(2 * NT - 1):
                    k0 = n * P if n < NT else CHUNK + (n - NT) * P
                    ins = nc.tensor.transpose(bank[4 + n // 4][:, (n % 4) * P:(n % 4 + 1) * P], z[:, AV, k0:k0 + P],
                                              ident[:, :])
                ins.then_inc(s["att_v_turned"], 1)

            def score(n):
                k0, kw = keys(n)
                if n:
                    pe.wait_ge(s["att_exped"], n)
                else:
                    pe.wait_ge(s["att_v_made"], 1)
                for u in range(2):
                    for kv in range(KV_HEADS):
                        rows = slice(kv * HD, (kv + 1) * HD)
                        ins = mm(bank[4 + kv][:, u * P:u * P + kw],
                                 zq[rows, n, 2 * u:2 * u + 2, :].rearrange("p c t -> p (c t)"),
                                 z[rows, AK, k0:k0 + kw], start=True, stop=True)
                ins.then_inc(s["att_scored"], 1)

            def turn_probs(n):
                _, kw = keys(n)
                pe.wait_ge(s["att_scaled"], n + 1)
                if n:
                    pe.wait_ge(s["att_p_made"], n)
                for j in range(4):
                    ins = nc.tensor.transpose(bank[6][0:kw, j * P:(j + 1) * P], probs[:, n % 2, j, 0:kw], ident[:, :])
                ins.then_inc(s["att_p_turned"], 1)

            def attend(n):
                _, kw = keys(n)
                pe.wait_ge(s["att_p_made"], n + 1)
                if n:
                    pe.wait_ge(s["att_kept"], n)
                v = att_vb[:, n // 2 - 1, :] if n and n % 2 == 0 else att_va[:, n // 2, :]
                for j in range(4):
                    kv = j // 2
                    ins = mm(bank[7][:, j * HD:(j + 1) * HD], probs_t[0:kw, n % 2, j, :],
                             v[0:kw, kv * HD:(kv + 1) * HD], start=True, stop=True)
                ins.then_inc(s["att_done"], 1)

            def attention(block):
                def beside(half):
                    n = att_step(block, half)
                    if n == -1:
                        turn_values()
                    if 0 <= n < NC:
                        score(n)
                    if 0 <= n - 3 < NC:
                        attend(n - 3)
                    if 0 <= n - 2 < NC:
                        turn_probs(n - 2)
                    if n == 20:
                        ml_score(0)
                return beside

            def ml_score(i):
                t = slice(i * P, (i + 1) * P)
                if i == 0:
                    pe.wait_ge(s["qk_made"], 4)
                    pe.wait_ge(s["z_evac"], ZT)
                else:
                    pe.wait_ge(s["ml_p_made"], i)
                for h in range(ML_HEADS):
                    rows = slice((h % 2) * 64, (h % 2) * 64 + 64)
                    ins = mm(bank[2 + h % 2][:, (h // 2) * P:(h // 2 + 1) * P], z[rows, MK + h // 2, t],
                             z[rows, MQ + h // 2, t], start=True, stop=True)
                ins.then_inc(s["ml_scored"], 1)
                if i:
                    pe.wait_ge(s["ml_k_made"], i)
                for r in range(2):
                    ins = nc.tensor.transpose(bank[4][:, r * P:(r + 1) * P], z[:, MK + r, t], ident[:, :])
                ins.then_inc(s["ml_k_turned"], 1)
                if i:
                    pe.wait_ge(s["ml_v_made"], i)
                for h in range(ML_HEADS):
                    ins = nc.tensor.transpose(bank[5][:, h * P:(h + 1) * P], z[:, MV + h, t], ident[:, :])
                ins.then_inc(s["ml_v_turned"], 1)

            def ml_turn_gate(i):
                if i:
                    pe.wait_ge(s["ml_gate_made"], i)
                else:
                    pe.wait_ge(s["z_evac"], ZT + 1)
                for h in range(ML_HEADS):
                    ins = nc.tensor.transpose(bank[6][:, h * P:(h + 1) * P], z[:, MO + h, i * P:(i + 1) * P],
                                              ident[:, :])
                ins.then_inc(s["ml_o_turned"], 1)

            def ml_state(i):
                pe.wait_ge(s["ml_k_made"], i + 1)
                pe.wait_ge(s["ml_v_made"], i + 1)
                if i:
                    pe.wait_ge(s["ml_state_made"], 2 * i)
                else:
                    pe.wait_ge(s["att_kept"], NC)
                for h in range(ML_HEADS):
                    rows = slice((h % 2) * 64, (h % 2) * 64 + 64)
                    ins = mm(bank[7][rows, (h // 2) * 256:(h // 2) * 256 + ML_V + 1],
                             ml_k[:, i % 2, h * ML_QK:(h + 1) * ML_QK], ml_v[:, i % 2, h, :], start=True, stop=True)
                if i == 0:
                    pe.wait_ge(s["att_squared"], NC)
                    ins = mm(bank[7][:, HALF - NC:], fold[:, :], sq_att[:, :], start=True, stop=True)
                ins.then_inc(s["ml_stated"], 1)

            def ml_sum(i):
                pe.wait_ge(s["ml_p_made"], i + 1)
                pe.wait_ge(s["ml_v_made"], i + 1)
                if i:
                    pe.wait_ge(s["ml_divided"], 2 * i)
                    pe.wait_ge(s["ml_state_made"], 2 * i)
                    pe.wait_ge(s["q_inter_made"], 2)
                for h in range(ML_HEADS):
                    rows = slice((h % 2) * 64, (h % 2) * 64 + 64)
                    c = (h % 2) * HALF + (h // 2) * (ML_V + 1)
                    dst = pz[0][:, c:c + ML_V + 1]
                    ins = mm(dst, ml_p[:, i % 2, h % 2, h // 2, :], ml_v[:, i % 2, h, :], start=True, stop=i == 0)
                    if i:
                        ins = mm(dst, q_inter[rows, h // 2, i * P:(i + 1) * P], state[rows, i % 2, h // 2, :],
                                 start=False, stop=True)
                ins.then_inc(s["ml_summed"], 1)

            def turn_mix(i):
                pe.wait_ge(s["mix_scaled"], i + 1)
                if i:
                    pe.wait_ge(s["mix_lo_made"], i)
                else:
                    pe.wait_ge(s["ml_p_made"], NT)
                for n in (2 * i, 2 * i + 1):
                    for kv in range(2):
                        dst = pz[1][:, 2 * kv * P:(2 * kv + 2) * P].rearrange("p (a t) -> p a t", a=2)
                        c = (n % 2) * CHUNK
                        nc.tensor.transpose(dst[:, :, c:c + CHUNK],
                                            zq[:, n, 2 * kv:2 * kv + 2, :].rearrange("p j d -> p (j d)"), ident[:, :])
                for h in range(ML_HEADS):
                    ins = nc.tensor.transpose(pz[1][:, (4 + h) * P:(5 + h) * P], z[:, MV + h, i * P:(i + 1) * P],
                                              ident[:, :])
                ins.then_inc(s["mix_turned"], 1)

            def out_project(i, beside):
                u = i % 2
                pe.wait_ge(s["mix_lo_made"], i + 1)
                for half in range(2):
                    n = 2 * i + half
                    if n >= 4:
                        pe.wait_ge(s["x1_added"], n - 3)
                    c = slice(half * HALF, (half + 1) * HALF)
                    for k in range(NK):
                        if half and k == NK // 2:
                            beside()
                        if n == 0:
                            pe.wait_ge(s["wo_split"], k + 1)
                        mm(bank[4 + n % 4], mix_hi[u][:, k, :], wo_hi[:, k, c], start=k == 0, stop=False)
                        mm(bank[4 + n % 4], mix_hi[u][:, k, :], wo_lo[:, k, c], start=False, stop=False)
                        ins = mm(bank[4 + n % 4], mix_lo[u][:, k, :], wo_hi[:, k, c], start=False, stop=k == NK - 1)
                    ins.then_inc(s["out_done"], 1)

            def turn_h2(i):
                pe.wait_ge(s["x1_scaled"], i + 1)
                if i:
                    pe.wait_ge(s["h2_f_made"], i)
                for k in range(NK):
                    ins = nc.tensor.transpose(h2_bank(i, k // 4)[:, k % 4 * P:(k % 4 + 1) * P],
                                              x_hat2[:, k * P:(k + 1) * P], ident[:, :])
                ins.then_inc(s["h2_turned"], 1)

            for b in range(ATT_BLOCK, ZT + 1):
                z_block(b, attention(b))

            ml_state(0)
            for i in range(NT):
                if i + 1 < NT:
                    ml_score(i + 1)
                ml_turn_gate(i)
                if i == NT - 1:
                    turn_mix(0)
                ml_sum(i)
                if i + 2 < NT:
                    ml_state(i + 1)

            for i in range(NT):
                if i + 1 < NT:
                    turn_mix(i + 1)

                def beside():
                    if i:
                        turn_h2(i - 1)

                out_project(i, beside)

            def up(g, m):
                pe.wait_ge(s["ffn_split"], 6 * g + m + 1)
                pe.wait_ge(s["conv_made"], 4 * g + m - 1)
                u = m % 2
                project(pz[u], w_hi[u], w_lo[u], h2).then_inc(s["up_done"], 1)

            def down_parts(dst, k, n, first, last):
                i, c = n // 2, slice((n % 2) * HALF, (n % 2 + 1) * HALF)
                ah, al = (v[:, k, i * P:(i + 1) * P] for v in (act_hi, act_lo))
                mm(dst, ah, wd_hi[:, k, c], start=first, stop=False)
                mm(dst, ah, wd_lo[:, k, c], start=False, stop=False)
                return mm(dst, al, wd_hi[:, k, c], start=False, stop=last)

            def down(g):
                pe.wait_ge(s["act_split"], 2 * g + 2)
                pe.wait_ge(s["ffn_split"], 6 * g + 6)
                for n in range(2 * NT):
                    if isinstance(g, int) and g == 0:
                        if n >= 4:
                            pe.wait_ge(s["down_added"], n - 3)
                    else:
                        pe.wait_ge(s["down_added"], 16 * g + n - 3)
                    for k in range(PAIRS):
                        ins = down_parts(bank[4 + n % 4], k, n, k == 0, k == PAIRS - 1)
                    ins.then_inc(s["down_done"], 1)

            def down_last(g):
                pe.wait_ge(s["act_split"], 2 * g + 1)
                pe.wait_ge(s["ffn_split"], 6 * g + 5)
                for n in range(8):
                    if n < 4:
                        pe.wait_ge(s["down_added"], 16 * g + n - 3)
                    else:
                        pe.wait_ge(s["conv_made"], 4 * g + 3 + (n - 4) // 2)
                    down_parts(last_bank(n), 0, n, True, False)
                pe.wait_ge(s["act_split"], 2 * g + 2)
                pe.wait_ge(s["ffn_split"], 6 * g + 6)
                for n in range(8):
                    down_parts(last_bank(n), 1, n, False, True).then_inc(s["down_done"], 1)
                for n in range(8, 16):
                    pe.wait_ge(s["down_added"], 16 * g + n - 7)
                    down_parts(last_bank(n), 0, n, True, False)
                    down_parts(last_bank(n), 1, n, False, True).then_inc(s["down_done"], 1)

            pe.wait_ge(s["h2_lo_made"], NT - 1)
            for m in range(2):
                pe.wait_ge(s["ffn_split"], m + 1)
                project(pz[m], w_hi[m], w_lo[m], h2, (0,))
                if m == 0:
                    turn_h2(NT - 1)
            pe.wait_ge(s["h2_lo_made"], NT)
            for m in range(2):
                project(pz[m], w_hi[m], w_lo[m], h2, (1,)).then_inc(s["up_done"], 1)
            up(0, 2)
            up(0, 3)
            up(1, 0)
            up(1, 1)
            down(0)
            up(1, 2)
            up(1, 3)
            with pe.Fori(2, GROUPS) as g:
                up(g, 0)
                up(g, 1)
                down(g - 1)
                up(g, 2)
                up(g, 3)
            down_last(GROUPS - 1)


_INS = ["x", "norm1_g", "w_in", "b_in", "w_qk_conv", "b_qk_conv", "attn_sinks", "g_att_out", "g_ml_out", "w_out",
        "norm2_g", "w_up", "w_ffn_conv", "b_ffn_conv", "w_down", "final_g"]
_OUT = ((1, S, D), "float32")


def kernel(**inputs):
    import numpy as _np
    import concourse.bacc as _bacc
    from concourse import mybir as _mybir
    from concourse.bass_utils import run_bass_kernel_spmd as _run

    nc = _bacc.Bacc("TRN2", target_bir_lowering=False, num_devices=1)
    arrays, args = {}, []
    for name in _INS:
        a = _np.ascontiguousarray(inputs[name])
        arrays[f"in_{name}"] = a
        args.append(nc.dram_tensor(f"in_{name}", a.shape, _mybir.dt.from_np(a.dtype), kind="ExternalInput").ap())
    out = nc.dram_tensor("out_0", _OUT[0], _mybir.dt.from_np(_np.dtype(_OUT[1])), kind="ExternalOutput").ap()
    hymba_kernel(nc, *args, out)
    r = _run(nc, [arrays], core_ids=[0])
    return r.results[0]["out_0"]
```
